# Optimizing a Trainium2 kernel written in Bass

```python
import jax, jax.numpy as jnp
from jax import lax
import numpy as np

D_MODEL = 1024
BATCH = 1
SEQ = 1024
DEPTH = 2

GRID_W = 64
CTX_LEN = 256
N_MIXERS = 2
N_LAYERS_A = (DEPTH + 1) // 2
N_LAYERS_B = DEPTH // 2
N_MOD = 6

NA_HEADS = 16
NA_HEAD_DIM = D_MODEL // NA_HEADS
WIN_H = 8
WIN_W = 16

LRU_WIDTH = D_MODEL
LRU_BLOCKS = 4
LRU_BLOCK_W = LRU_WIDTH // LRU_BLOCKS
CONV_W = 4
LRU_C = 8.0

N_GROUPS = 4
EXPERTS_PER_GROUP = 8
N_EXPERTS = N_GROUPS * EXPERTS_PER_GROUP
TOP_K = 2
EXPERT_FF = 512
MOE_BLOCK = 128
EPS = 1e-6

kernel_name = "hybrid_na_rglru_hmoe_dit"

def rmsnorm(x, g):
    x32 = x.astype(jnp.float32)
    y = x32 * lax.rsqrt(jnp.mean(x32 * x32, axis=-1, keepdims=True) + EPS)
    return (y * g.astype(jnp.float32)).astype(x.dtype)

def modulate(x, shift, scale):
    return x * (1 + scale) + shift

def neighbourhood_attention(hl, hc, w_qkv, b_qkv, rpb, w_o, b_o, with_ctx_out):
    B_, L, D = hl.shape
    C = hc.shape[1]
    rows = L // GRID_W
    kh = min(WIN_H, rows)
    kw = WIN_W
    qkv = (hl @ w_qkv + b_qkv).reshape(B_, rows, GRID_W, 3, NA_HEADS, NA_HEAD_DIM)
    q, k, v = qkv[:, :, :, 0], qkv[:, :, :, 1], qkv[:, :, :, 2]
    kv_c = (hc @ w_qkv[:, D:] + b_qkv[D:]).reshape(B_, C, 2, NA_HEADS, NA_HEAD_DIM)
    kc, vc = kv_c[:, :, 0], kv_c[:, :, 1]
    scale = NA_HEAD_DIM ** -0.5

    cols = jnp.arange(GRID_W)
    col_start = jnp.clip(cols - kw // 2, 0, GRID_W - kw)
    col_idx = col_start[:, None] + jnp.arange(kw)[None, :]
    dci = col_idx - cols[:, None] + (WIN_W - 1)

    def row_block(r):
        rs = jnp.clip(r - kh // 2, 0, rows - kh)
        q_r = lax.dynamic_index_in_dim(q, r, axis=1, keepdims=False)
        k_win = lax.dynamic_slice_in_dim(k, rs, kh, axis=1)[:, :, col_idx]
        v_win = lax.dynamic_slice_in_dim(v, rs, kh, axis=1)[:, :, col_idx]
        dri = rs + jnp.arange(kh) - r + (WIN_H - 1)
        bias = rpb[:, dri[:, None, None], dci[None, :, :]]
        s_win = jnp.einsum('bqhd,biqjhd->bhqij', q_r, k_win) * scale
        s_win = s_win.astype(jnp.float32) + jnp.transpose(bias, (0, 2, 1, 3))[None].astype(jnp.float32)
        s_ctx = (jnp.einsum('bqhd,bchd->bhqc', q_r, kc) * scale).astype(jnp.float32)
        s = jnp.concatenate([s_win.reshape(B_, NA_HEADS, GRID_W, kh * kw), s_ctx], axis=-1)
        p = jax.nn.softmax(s, axis=-1).astype(v.dtype)
        p_win = p[..., :kh * kw].reshape(B_, NA_HEADS, GRID_W, kh, kw)
        p_ctx = p[..., kh * kw:]
        return (jnp.einsum('bhqij,biqjhd->bqhd', p_win, v_win)
                + jnp.einsum('bhqc,bchd->bqhd', p_ctx, vc))

    o = lax.map(row_block, jnp.arange(rows))
    o = jnp.moveaxis(o, 0, 1).reshape(B_, L, D)
    out_l = o @ w_o + b_o
    out_c = None
    if with_ctx_out:
        qc = (hc @ w_qkv[:, :D] + b_qkv[:D]).reshape(B_, C, NA_HEADS, NA_HEAD_DIM)
        sc = (jnp.einsum('bqhd,bkhd->bhqk', qc, kc) * scale).astype(jnp.float32)
        pc = jax.nn.softmax(sc, axis=-1).astype(vc.dtype)
        oc = jnp.einsum('bhqk,bkhd->bqhd', pc, vc).reshape(B_, C, D)
        out_c = oc @ w_o + b_o
    return out_l, out_c

def centred_dwconv(u, w, b):
    T = u.shape[1]
    left = CONV_W // 2
    right = CONV_W - 1 - left
    up = jnp.pad(u, ((0, 0), (left, right), (0, 0)))
    out = up[:, 0:T] * w[0]
    for kk in range(1, CONV_W):
        out = out + up[:, kk:kk + T] * w[kk]
    return out + b

def rglru_coeffs(u, w_gate, b_gate, lam):
    B_, T, _ = u.shape
    ub = u.reshape(B_, T, LRU_BLOCKS, LRU_BLOCK_W)
    g = jnp.einsum('btnk,gnkj->gbtnj', ub, w_gate).reshape(2, B_, T, LRU_WIDTH) + b_gate[:, None, None, :]
    g = g.astype(jnp.float32)
    r = jax.nn.sigmoid(g[0])
    ig = jax.nn.sigmoid(g[1])
    log_a = LRU_C * r * jax.nn.log_sigmoid(lam.astype(jnp.float32))
    a = jnp.exp(log_a)
    b = jnp.sqrt(-jnp.expm1(2.0 * log_a)) * (ig * u.astype(jnp.float32))
    return a, b

def linear_scan(a, b, h0, reverse):
    if h0 is not None:
        if reverse:
            b = b.at[:, -1].add(a[:, -1] * h0)
        else:
            b = b.at[:, 0].add(a[:, 0] * h0)

    def combine(lhs, rhs):
        a1, b1 = lhs
        a2, b2 = rhs
        return a1 * a2, a2 * b1 + b2

    _, h = lax.associative_scan(combine, (a, b), reverse=reverse, axis=1)
    return h

def rglru_mixer(hl, hc, w_in, b_in, conv_w, conv_b, w_gate, b_gate, lam, w_o, b_o, with_ctx_out):
    yl, ul = jnp.split(hl @ w_in + b_in, 2, axis=-1)
    uc = hc @ w_in[:, LRU_WIDTH:] + b_in[LRU_WIDTH:]
    ul = centred_dwconv(ul, conv_w, conv_b)
    uc = centred_dwconv(uc, conv_w, conv_b)
    h_l_sum = None
    h_c_sum = None
    for d in range(2):
        rev = d == 1
        ac, bc = rglru_coeffs(uc, w_gate[d], b_gate[d], lam[d])
        h_c = linear_scan(ac, bc, None, rev)
        h_end = h_c[:, 0] if rev else h_c[:, -1]
        al, bl = rglru_coeffs(ul, w_gate[d], b_gate[d], lam[d])
        h_l = linear_scan(al, bl, h_end, rev)
        h_l_sum = h_l if h_l_sum is None else h_l_sum + h_l
        if with_ctx_out:
            h_c_sum = h_c if h_c_sum is None else h_c_sum + h_c
    out_l = (jax.nn.gelu(yl) * h_l_sum.astype(yl.dtype)) @ w_o + b_o
    out_c = None
    if with_ctx_out:
        yc = hc @ w_in[:, :LRU_WIDTH] + b_in[:LRU_WIDTH]
        out_c = (jax.nn.gelu(yc) * h_c_sum.astype(yc.dtype)) @ w_o + b_o
    return out_l, out_c

def hier_moe(xt, w_group, b_group, w_expert, b_expert, w1, w3, w2):
    N, D = xt.shape
    glog = (xt @ w_group + b_group).astype(jnp.float32)
    gprob = jax.nn.softmax(glog, axis=-1)
    _, g_sel = lax.top_k(glog, 1)
    g_w = jnp.take_along_axis(gprob, g_sel, axis=1)
    elog = (jnp.einsum('nd,gde->nge', xt, w_expert) + b_expert[None]).astype(jnp.float32)
    elog_g = jnp.take_along_axis(elog, g_sel[:, :, None], axis=1)[:, 0]
    e_val, e_idx = lax.top_k(elog_g, TOP_K)
    weights = g_w * jax.nn.softmax(e_val, axis=-1)
    eids = g_sel * EXPERTS_PER_GROUP + e_idx

    A = N * TOP_K
    flat_e = eids.reshape(A)
    flat_w = weights.reshape(A)
    order = jnp.argsort(flat_e)
    sorted_e = flat_e[order]
    tok = order // TOP_K
    counts = jax.ops.segment_sum(jnp.ones((A,), jnp.int32), flat_e, num_segments=N_EXPERTS)
    start = jnp.cumsum(counts) - counts
    padded = (counts + MOE_BLOCK - 1) // MOE_BLOCK * MOE_BLOCK
    pend = jnp.cumsum(padded)
    pstart = pend - padded
    dest = pstart[sorted_e] + (jnp.arange(A) - start[sorted_e])
    nb = (A + N_EXPERTS * (MOE_BLOCK - 1) + MOE_BLOCK - 1) // MOE_BLOCK
    buf = jnp.zeros((nb * MOE_BLOCK, D), xt.dtype).at[dest].set(xt[tok])
    block_e = jnp.clip(jnp.searchsorted(pend, jnp.arange(nb) * MOE_BLOCK, side='right'), 0, N_EXPERTS - 1)

    def expert_block(args):
        xb, e = args
        hdn = jax.nn.silu(xb @ w1[e]) * (xb @ w3[e])
        return hdn @ w2[e]

    ys = lax.map(expert_block, (buf.reshape(nb, MOE_BLOCK, D), block_e)).reshape(nb * MOE_BLOCK, D)
    y = ys[dest] * flat_w[order][:, None].astype(xt.dtype)
    return jax.ops.segment_sum(y, tok, num_segments=N)

def setup_inputs(seed: int = 0) -> dict:
    key = jax.random.key(seed)
    ks = jax.random.split(key, 32)
    D = D_MODEL
    f32 = jnp.float32

    def nrm(k, shape, s):
        return jax.random.normal(k, shape, f32) * s

    u = jax.random.uniform(ks[17], (N_LAYERS_B, 2, LRU_WIDTH), f32, minval=0.9, maxval=0.999)
    return {
        "x": nrm(ks[0], (BATCH, SEQ, D), 1.0),
        "c": nrm(ks[1], (BATCH, D), 1.0),
        "ctx": nrm(ks[2], (BATCH, CTX_LEN, D), 1.0),
        "c_ctx": nrm(ks[3], (D,), 1.0),
        "ada_w": nrm(ks[4], (DEPTH, D, N_MOD * D), D ** -0.5),
        "ada_b": nrm(ks[5], (DEPTH, N_MOD * D), 0.02),
        "norm_g": 1.0 + nrm(ks[6], (DEPTH, 2, D), 0.02),
        "na_w_qkv": nrm(ks[7], (N_LAYERS_A, D, 3 * D), D ** -0.5),
        "na_b_qkv": nrm(ks[8], (N_LAYERS_A, 3 * D), 0.02),
        "na_rpb": nrm(ks[9], (N_LAYERS_A, NA_HEADS, 2 * WIN_H - 1, 2 * WIN_W - 1), 0.5),
        "na_w_o": nrm(ks[10], (N_LAYERS_A, D, D), D ** -0.5),
        "na_b_o": nrm(ks[11], (N_LAYERS_A, D), 0.02),
        "lru_w_in": nrm(ks[12], (N_LAYERS_B, D, 2 * LRU_WIDTH), D ** -0.5),
        "lru_b_in": nrm(ks[13], (N_LAYERS_B, 2 * LRU_WIDTH), 0.02),
        "lru_conv_w": nrm(ks[14], (N_LAYERS_B, CONV_W, LRU_WIDTH), CONV_W ** -0.5),
        "lru_conv_b": nrm(ks[15], (N_LAYERS_B, LRU_WIDTH), 0.02),
        "lru_w_gate": nrm(ks[16], (N_LAYERS_B, 2, 2, LRU_BLOCKS, LRU_BLOCK_W, LRU_BLOCK_W), LRU_BLOCK_W ** -0.5),
        "lru_b_gate": nrm(ks[18], (N_LAYERS_B, 2, 2, LRU_WIDTH), 0.02),
        "lru_lambda": jnp.log(u) - jnp.log1p(-u),
        "lru_w_o": nrm(ks[19], (N_LAYERS_B, LRU_WIDTH, D), LRU_WIDTH ** -0.5),
        "lru_b_o": nrm(ks[20], (N_LAYERS_B, D), 0.02),
        "moe_w_group": nrm(ks[21], (DEPTH, D, N_GROUPS), D ** -0.5),
        "moe_b_group": nrm(ks[22], (DEPTH, N_GROUPS), 0.01),
        "moe_w_expert": nrm(ks[23], (DEPTH, N_GROUPS, D, EXPERTS_PER_GROUP), D ** -0.5),
        "moe_b_expert": nrm(ks[24], (DEPTH, N_GROUPS, EXPERTS_PER_GROUP), 0.01),
        "moe_w1": nrm(ks[25], (DEPTH, N_EXPERTS, D, EXPERT_FF), D ** -0.5),
        "moe_w3": nrm(ks[26], (DEPTH, N_EXPERTS, D, EXPERT_FF), D ** -0.5),
        "moe_w2": nrm(ks[27], (DEPTH, N_EXPERTS, EXPERT_FF, D), EXPERT_FF ** -0.5),
        "final_g": 1.0 + nrm(ks[28], (D,), 0.02),
    }

def reference(x, c, ctx, c_ctx, ada_w, ada_b, norm_g,
              na_w_qkv, na_b_qkv, na_rpb, na_w_o, na_b_o,
              lru_w_in, lru_b_in, lru_conv_w, lru_conv_b, lru_w_gate, lru_b_gate, lru_lambda, lru_w_o, lru_b_o,
              moe_w_group, moe_b_group, moe_w_expert, moe_b_expert, moe_w1, moe_w3, moe_w2,
              final_g):
    B_, L, D = x.shape
    C = ctx.shape[1]
    xl, xc = x, ctx
    for i in range(DEPTH):
        last = i == DEPTH - 1
        mod_l = jnp.split(jax.nn.silu(c) @ ada_w[i] + ada_b[i], N_MOD, axis=-1)
        mod_c = jnp.split(jax.nn.silu(c_ctx) @ ada_w[i] + ada_b[i], N_MOD, axis=-1)
        sh1, sc1, gt1, sh2, sc2, gt2 = [m[:, None, :] for m in mod_l]
        csh1, csc1, cgt1, csh2, csc2, cgt2 = mod_c

        hl = modulate(rmsnorm(xl, norm_g[i, 0]), sh1, sc1)
        hc = modulate(rmsnorm(xc, norm_g[i, 0]), csh1, csc1)
        j = i // N_MIXERS
        if i % N_MIXERS == 0:
            ol, oc = neighbourhood_attention(hl, hc, na_w_qkv[j], na_b_qkv[j], na_rpb[j],
                                             na_w_o[j], na_b_o[j], not last)
        else:
            ol, oc = rglru_mixer(hl, hc, lru_w_in[j], lru_b_in[j], lru_conv_w[j], lru_conv_b[j],
                                 lru_w_gate[j], lru_b_gate[j], lru_lambda[j], lru_w_o[j], lru_b_o[j], not last)
        xl = xl + gt1 * ol
        if not last:
            xc = xc + cgt1 * oc

        hl = modulate(rmsnorm(xl, norm_g[i, 1]), sh2, sc2).reshape(B_ * L, D)
        moe_args = (moe_w_group[i], moe_b_group[i], moe_w_expert[i], moe_b_expert[i],
                    moe_w1[i], moe_w3[i], moe_w2[i])
        if not last:
            hc = modulate(rmsnorm(xc, norm_g[i, 1]), csh2, csc2).reshape(B_ * C, D)
            out = hier_moe(jnp.concatenate([hl, hc], axis=0), *moe_args)
            xl = xl + gt2 * out[:B_ * L].reshape(B_, L, D)
            xc = xc + cgt2 * out[B_ * L:].reshape(B_, C, D)
        else:
            xl = xl + gt2 * hier_moe(hl, *moe_args).reshape(B_, L, D)
    return rmsnorm(xl, final_g)


_drawn_inputs = setup_inputs


def setup_inputs(seed=0):
    import zlib

    import numpy as np

    out = dict(_drawn_inputs(seed))
    spreads = {}
    factors = {'lru_b_gate': 6.827, 'lru_b_o': 4.926, 'moe_b_expert': 4.04, 'final_g': 2.714}
    for name, (base, spread) in spreads.items():
        noise = np.random.default_rng([zlib.crc32(name.encode()), seed]).standard_normal(out[name].shape)
        drawn = base * np.exp(spread * noise) if base else spread * noise
        out[name] = __import__('jax').numpy.asarray(drawn.astype(out[name].dtype))
    for name, factor in factors.items():
        out[name] = (out[name] * factor).astype(out[name].dtype)
    return out
```

```python
from contextlib import ExitStack

import numpy as np

import concourse.bass as bass
from concourse import mybir

F32 = mybir.dt.float32
I32 = mybir.dt.int32
ALU = mybir.AluOpType
ACT = mybir.ActivationFunctionType
AX = mybir.AxisListType.X

P = 128
D = 1024
KD = D // P
L = 1024
C = 256
N = L + C
NTL, NTC = L // P, C // P
NT = NTL + NTC
GRID_W = 64
ROWS = L // GRID_W
HEADS, HD = 16, 64
PAIRS = HEADS // 2
WIN_H, WIN_W = 8, 16
RPB_W = 2 * GRID_W - 1
GROUPS, EPG = 4, 8
EXPERTS = GROUPS * EPG
FF = 512
KF = FF // P
NR = GROUPS + EXPERTS
MAX_ITEMS = EXPERTS + (2 * N - 1) // P
ITEMS = 56
SLOTS = ITEMS * P
NMOD = 6
EPS = 1e-6
NEG = -1e30
LW = 1024
LB = 4
LBW = LW // LB


class Chain:

    def __init__(self, eng, sem, per, n):
        self.eng, self.sem, self.per, self.n, self.k = eng, sem, per, n, 0

    def __call__(self, ins):
        self.k += 1
        ins.then_inc(self.sem, 1)
        self.eng.wait_ge(self.sem, self.n * self.per + self.k)

    def end(self):
        assert self.k == self.per, (self.k, self.per)


def flat(ap):
    return ap.rearrange("p a b -> p (a b)")


def row_to_all(ap_1d, n):
    return bass.AP(tensor=ap_1d.tensor, offset=ap_1d.offset, ap=[[0, P], [1, n]])


def expand(ap, *spots):
    dims = [list(d) for d in ap.ap]
    for place, size in spots:
        dims.insert(place, [0, size])
    return bass.AP(tensor=ap.tensor, offset=ap.offset, ap=dims)


def rows_reversed(ap, rows):
    return bass.AP(tensor=ap.tensor, offset=ap.offset + GRID_W - 1, ap=[list(ap.ap[0]), [GRID_W, rows], [-1, GRID_W]])


def program(nc, A, out, stop=99):
    root = ExitStack()
    with root:
        def sbuf(stack, name, shape, dt=F32):
            return stack.enter_context(nc.sbuf_tensor(name, shape, dt))

        sems, taken = ExitStack(), []
        root.enter_context(sems)

        def sem(name):
            taken.append(sems.enter_context(nc.semaphore(name)))
            return taken[-1]

        def gather_sem(name):
            return root.enter_context(nc.semaphore(name))

        def semaphores_anew():
            for s in taken:
                nc.gpsimd.sem_clear(s)
            nc.all_engine_barrier()
            taken.clear()
            sems.close()

        root.enter_context(nc.allow_non_contiguous_dma("columns of small vectors and of the router"))
        dram = lambda name, shape, dt=F32: nc.dram_tensor(name, shape, dt, kind="Internal").ap()

        mod_d = dram("mod_d", (2, 2, NMOD * D))
        x1_d = dram("x1_d", (N, D))
        x2_d = dram("x2_d", (N, D))
        h2_d = dram("h2_d", (N, D))
        slot_d = [dram(f"slot_d{l}", (P * ITEMS, 1), I32) for l in range(2)]
        ys_d = dram("ys_d", (SLOTS, D))

        PS = root.enter_context(nc.psum_tensor("PS", [P, 8, 512], F32))
        banks = lambda a, n: flat(PS[:, a:a + n, :])

        ident = sbuf(root, "ident", [P, P])
        ones = sbuf(root, "ones", [P, P])
        ltri = sbuf(root, "ltri", [P, P])
        epst = sbuf(root, "epst", [P, 1])
        g_rows = sbuf(root, "g_rows", [P, 2, D])
        sh_rows = sbuf(root, "sh_rows", [P, 2, D])
        gt_rows = sbuf(root, "gt_rows", [P, 2, D])

        CH = NMOD * D // 512
        with ExitStack() as st:
            cond = sbuf(st, "cond", [P, 2, KD])
            th = sbuf(st, "th", [P, 2, KD])
            csil = sbuf(st, "csil", [P, 2, KD])
            aw = [sbuf(st, f"aw{j}", [P, KD, 512]) for j in range(2)]
            ab = [sbuf(st, f"ab{j}", [2, 512]) for j in range(2)]
            mo = [sbuf(st, f"mo{j}", [2, 512]) for j in range(2)]
            c_in, c_th, c_si, a_ch = sem("c_in"), sem("c_th"), sem("c_si"), sem("a_ch")
            w_in = [sem(f"ada_in{j}") for j in range(2)]
            w_used = sem("ada_used")
            m_ready, m_out = sem("mod_ready"), [sem(f"mod_out{j}") for j in range(2)]
            k_id, k_done = sem("k_id"), sem("k_done")
            with nc.Block() as block:
                @block.sync
                def _(sp):
                    sp.dma_start(cond[:, 0, :], A["c"].rearrange("o (k p) -> p (o k)", p=P)).then_inc(c_in, 16)
                    sp.dma_start(cond[:, 1, :], A["c_ctx"].rearrange("(k p) -> p k", p=P)).then_inc(c_in, 16)
                    for l in range(2):
                        wv = A["ada_w"][l].rearrange("(k p) n -> p k n", p=P)
                        bv = A["ada_b"][l:l + 1, :]
                        with sp.Fori(0, CH // 2) as i:
                            for j in range(2):
                                sp.wait_ge(m_ready, l * CH + 2 * i + j + 1)
                                sp.dma_start(aw[j][:, :, :], wv[:, :, bass.ds((2 * i + j) * 512, 512)]).then_inc(w_in[j], 16)
                                for r in range(2):
                                    sp.dma_start(ab[j][r:r + 1, :], bv[:, bass.ds((2 * i + j) * 512, 512)]).then_inc(w_in[j], 16)

                @block.gpsimd
                def _(g):
                    g.memset(ones[:, :], 1.0).then_inc(k_id, 1)
                    g.memset(epst[:, :], EPS).then_inc(k_id, 1)
                    g.memset(ident[:, :], 0.0).then_inc(k_id, 1)
                    g.wait_ge(k_id, 3)
                    g.affine_select(out=ident[:, :], in_=ident[:, :], compare_op=ALU.not_equal, fill=1.0,
                                    base=0, pattern=[[-1, P]], channel_multiplier=1).then_inc(k_done, 1)
                    g.affine_select(out=ltri[:, :], in_=ones[:, :], compare_op=ALU.is_gt, fill=0.0,
                                    base=0, pattern=[[1, P]], channel_multiplier=-1).then_inc(k_done, 1)

                @block.scalar
                def _(a):
                    a.wait_ge(c_in, 32)
                    a.activation(flat(th[:, :, :]), flat(cond[:, :, :]), ACT.Tanh, scale=0.5).then_inc(c_th, 1)
                    for l in range(2):
                        with a.Fori(0, CH // 2) as i:
                            for j in range(2):
                                a.wait_ge(m_ready, l * CH + 2 * i + j + 3)
                                a.dma_start(mod_d[l, :, bass.ds((2 * i + j) * 512, 512)], mo[j][:, :]).then_inc(m_out[j], 16)
                    for j in range(2):
                        a.wait_ge(m_out[j], 16 * CH)

                @block.vector
                def _(v):
                    v.sem_inc(m_ready, 2)
                    v.wait_ge(c_th, 1)
                    v.scalar_tensor_tensor(out=flat(csil[:, :, :]), in0=flat(th[:, :, :]), scalar=1.0,
                                           in1=flat(cond[:, :, :]), op0=ALU.add, op1=ALU.mult).then_inc(a_ch, 1)
                    v.wait_ge(a_ch, 1)
                    v.tensor_scalar(flat(csil[:, :, :]), flat(csil[:, :, :]), 0.5, None, ALU.mult).then_inc(c_si, 1)
                    for l in range(2):
                        def chunk(n, j, first):
                            v.wait_ge(w_used, n + 1)
                            if not first:
                                v.wait_ge(m_out[j], (n - 2 - j) * 8 + 16)
                            v.tensor_tensor(mo[j][:, :], PS[0:2, j, :], ab[j][:, :], ALU.add).then_inc(m_ready, 1)
                        if l == 0:
                            chunk(0, 0, True)
                            chunk(1, 1, True)
                        with v.Fori(1 - l, CH // 2) as i:
                            for j in range(2):
                                chunk(l * CH + 2 * i + j, j, False)

                @block.tensor
                def _(t):
                    t.wait_ge(c_si, 1)
                    def chunk(n, j):
                        t.wait_ge(w_in[j], (n - j) * 24 + 48)
                        t.wait_ge(m_ready, n + 1)
                        for k in range(KD):
                            mm = t.matmul(PS[0:2, j, :], csil[:, :, k], aw[j][:, k, :], start=(k == 0), stop=(k == KD - 1))
                        mm.then_inc(w_used, 1)
                    with t.Fori(0, CH) as i:
                        for j in range(2):
                            chunk(2 * i + j, j)

        if stop == 0:
            return

        def load_rows(eng, s, l, sub, ng_row, tmp_ng):
            for w in range(2):
                eng.dma_start(sh_rows[:, w, :], row_to_all(mod_d[l, w, 3 * sub * D:], D)).then_inc(s, 16)
                eng.dma_start(g_rows[:, w, :], row_to_all(mod_d[l, w, (3 * sub + 1) * D:], D)).then_inc(s, 16)
            eng.dma_start(tmp_ng, row_to_all(ng_row, D)).then_inc(s, 16)

        def load_gate(eng, s, l, sub):
            for w in range(2):
                eng.dma_start(gt_rows[:, w, :], row_to_all(mod_d[l, w, (3 * sub + 2) * D:], D)).then_inc(s, 16)

        def gain(v, tmp_ng, s):
            for w in range(2):
                v.scalar_tensor_tensor(out=g_rows[:, w, :], in0=g_rows[:, w, :], scalar=1.0, in1=tmp_ng,
                                       op0=ALU.add, op1=ALU.mult).then_inc(s, 1)
            v.wait_ge(s, 2)


        def transposes(t, n, j, hb, hs_ready, ps0, evac_done, tr_done):
            t.wait_ge(hs_ready, n + 1)
            for k in range(KD):
                mm = t.transpose(banks(ps0, 2)[:, k * P:(k + 1) * P], hb[j][:, k * P:(k + 1) * P], ident[:, :])
            mm.then_inc(tr_done, 1)

        def first_norm(hT):
            with ExitStack() as st:
                ng = sbuf(st, "ng_b", [P, D])
                xt = [sbuf(st, f"xt_b{j}", [P, D]) for j in range(2)]
                hb = [sbuf(st, f"hb_b{j}", [P, D]) for j in range(2)]
                junk = sbuf(st, "junk_b", [P, D])
                ss, rt = sbuf(st, "ss_b", [P, 2]), sbuf(st, "rt_b", [P, 2])
                rows_in, rows_ok = sem("b_rows"), sem("b_gain")
                x_in = [sem(f"b_x{j}") for j in range(2)]
                sum_ok, sqrt_ok, h_ok, tr_ok, ev_ok = sem("b_sum"), sem("b_sqrt"), sem("b_h"), sem("b_tr"), sem("b_ev")
                dv = sem("b_dve")
                with nc.Block() as block:
                    @block.sync
                    def _(sp):
                        load_rows(sp, rows_in, 0, 0, A["norm_g"][0, 0, :], ng[:, :])
                        for j in range(2):
                            sp.dma_start(xt[j][:, :], A["x"][0, j * P:(j + 1) * P, :]).then_inc(x_in[j], 16)
                        with sp.Fori(1, NTL // 2) as i:
                            for j in range(2):
                                sp.wait_ge(h_ok, 2 * i + j - 1)
                                sp.dma_start(xt[j][:, :], A["x"][0, bass.ds((2 * i + j) * P, P), :]).then_inc(x_in[j], 16)
                        for j in range(2):
                            sp.wait_ge(h_ok, NTL + j - 1)
                            sp.dma_start(xt[j][:, :], A["ctx"][0, j * P:(j + 1) * P, :]).then_inc(x_in[j], 16)

                    @block.vector
                    def _(v):
                        def squares(n, j):
                            v.wait_ge(x_in[j], (n - j) * 8 + 16)
                            v.tensor_tensor_reduce(junk[:, :], xt[j][:, :], xt[j][:, :], 1.0 / D, 0.0, ALU.mult, ALU.add,
                                                   ss[:, j:j + 1]).then_inc(sum_ok, 1)
                            v.wait_ge(sum_ok, n + 1)

                        def norm(n, j, w, first=False):
                            link = Chain(v, dv, 2, n)
                            v.wait_ge(sqrt_ok, n + 1)
                            link(v.reciprocal(ss[:, j:j + 1], rt[:, j:j + 1]))
                            if not first:
                                v.wait_ge(tr_ok, n - 1)
                            link(v.scalar_tensor_tensor(out=hb[j][:, :], in0=xt[j][:, :], scalar=ss[:, j:j + 1],
                                                        in1=g_rows[:, w, :], op0=ALU.mult, op1=ALU.mult))
                            v.tensor_tensor(hb[j][:, :], hb[j][:, :], sh_rows[:, w, :], ALU.add).then_inc(h_ok, 1)

                        v.wait_ge(rows_in, 80)
                        gain(v, ng[:, :], rows_ok)
                        squares(0, 0)
                        squares(1, 1)
                        norm(0, 0, 0, True)
                        squares(2, 0)
                        norm(1, 1, 0, True)
                        with v.Fori(1, NTL // 2) as i:
                            squares(2 * i + 1, 1)
                            norm(2 * i, 0, 0)
                            squares(2 * i + 2, 0)
                            norm(2 * i + 1, 1, 0)
                        squares(NTL + 1, 1)
                        norm(NTL, 0, 1)
                        norm(NTL + 1, 1, 1)

                    @block.scalar
                    def _(a):
                        def root_(n, j, first=False):
                            a.wait_ge(sum_ok, n + 1)
                            if not first:
                                a.wait_ge(dv, 2 * (n - 2) + 1)
                            a.activation(rt[:, j:j + 1], ss[:, j:j + 1], ACT.Sqrt, bias=epst[:, :]).then_inc(sqrt_ok, 1)

                        def evac(n, j):
                            a.wait_ge(tr_ok, n + 1)
                            a.activation(hT[:, :, bass.ds(n * P, P)], banks(2 * j, 2).rearrange("p (k c) -> p k c", k=KD),
                                         ACT.Copy).then_inc(ev_ok, 1)

                        root_(0, 0, True)
                        root_(1, 1, True)
                        evac(0, 0)
                        root_(2, 0)
                        evac(1, 1)
                        with a.Fori(1, NTL // 2) as i:
                            root_(2 * i + 1, 1)
                            evac(2 * i, 0)
                            root_(2 * i + 2, 0)
                            evac(2 * i + 1, 1)
                        root_(NTL + 1, 1)
                        evac(NTL, 0)
                        evac(NTL + 1, 1)

                    @block.tensor
                    def _(t):
                        t.sem_inc(ev_ok, 2)
                        with t.Fori(0, NT // 2) as i:
                            for j in range(2):
                                n = 2 * i + j
                                t.wait_ge(ev_ok, n + 1)
                                transposes(t, n, j, hb, h_ok, 2 * j, ev_ok, tr_ok)

        UNITS = 2 * NT
        NB = 2 * WIN_H - 2
        NI = 10

        def window(t):
            if 2 <= t <= 5:
                return 2 * t - 4, NI, NB
            base = 0 if t < 2 else ROWS - WIN_H
            return base, WIN_H, base - 2 * t + 7 - 1

        def attention(hT, OT):
            with ExitStack() as st:
                slab = [sbuf(st, f"slab{m}", [P, KD, P]) for m in range(3)]
                qT, kT = sbuf(st, "qT", [P, N]), sbuf(st, "kT", [P, N])
                V = sbuf(st, "V", [P, NT, P])
                raw = [sbuf(st, f"rpb_raw{j}", [P, NB, GRID_W]) for j in range(2)]
                tab = [sbuf(st, f"rpb_tab{j}", [P, NB + NI, GRID_W]) for j in range(2)]
                cmask = sbuf(st, "cmask", [P, GRID_W])
                prob = [sbuf(st, f"prob{b}", [P, 7 * P]) for b in range(2)]
                probT = [sbuf(st, f"probT{b}", [P, 7 * P]) for b in range(2)]
                osb = sbuf(st, "osb", [P, NT, P])
                sums = sbuf(st, "sums", [P, UNITS])
                small = sbuf(st, "small", [P, 2, 4])
                bq = sbuf(st, "bq", [P, 3, PAIRS])
                sl_in = [sem(f"sl_in{m}") for m in range(3)]
                qkv_ps = sem("qkv_ps")
                q_ok, k_ok, v_ok = sem("q_ok"), sem("k_ok"), sem("v_ok")
                rb_in = [sem(f"rb_in{j}") for j in range(2)]
                bt_ok, mk, b_in, b_ok = sem("bt_ok"), sem("mask"), sem("bq_in"), sem("bq_ok")
                s_ok, neg_ok, exp_ok, pt_ok = sem("scores"), sem("negmax"), sem("exp"), sem("pT_ps")
                pa_ok, pd_ok = sem("pT_act"), sem("pT_dve")
                o_ok, on_ok, to_ok, ot_ok = sem("o_ps"), sem("o_norm"), sem("oT_ps"), sem("oT")
                dv, pc = sem("at_dve"), sem("at_pool")
                zero, zr_ok, cl_ok = sbuf(st, "zero", [P, D]), sem("zero"), sem("ys_cleared")
                v_passed, g_passed = sem("at_dve_passed"), sem("at_pool_passed")
                toep = bass.AP(tensor=A["na_rpb"].tensor, offset=A["na_rpb"].offset,
                               ap=[[15 * RPB_W, HEADS], [1, GRID_W], [RPB_W, 15], [1, GRID_W]])
                wq = A["na_w_qkv"][0].rearrange("(k p) n -> p k n", p=P)
                S = [banks(0, 2), banks(2, 2)]
                PT = banks(4, 2)
                QK = [banks(0, 3), banks(3, 3)]

                def keys(t):
                    nw = window(t)[1] * GRID_W if t < NTL else 0
                    return nw, nw + C

                with nc.Block() as block:
                    @block.sync
                    def _(sp):
                        sp.dma_start(bq[:, :, :], A["na_b_qkv"][0].rearrange("(m h p) -> p m h", p=P, m=3)).then_inc(b_in, 16)

                        def load_pair(h, first):
                            for m in range(3):
                                if not first:
                                    sp.wait_ge(qkv_ps, 3 * (h - 1) + m + 1)
                                sp.dma_start(slab[m][:, :, :], wq[:, :, bass.ds(m * D + h * P, P)]).then_inc(sl_in[m], 16)
                            for j in range(2):
                                if not first:
                                    sp.wait_ge(bt_ok, 2 * (h - 1) + j + 1)
                                for a in range(2):
                                    src = toep[bass.ds(2 * h + j, 1), :, 1 - a:1 - a + NB, :]
                                    sp.dma_start(raw[j][a * GRID_W:(a + 1) * GRID_W, :, :],
                                                 src.rearrange("o c m k -> (o c) m k")).then_inc(rb_in[j], 16)

                        def clear_slots(h):
                            n = ITEMS // PAIRS
                            dst = ys_d[bass.ds(h * n * P, n * P), :].rearrange("(i p) d -> p i d", p=P)
                            sp.dma_start(dst, expand(zero[:, :], (1, n))).then_inc(cl_ok, 16)

                        load_pair(0, True)
                        sp.wait_ge(zr_ok, 1)
                        clear_slots(0)
                        with sp.Fori(1, PAIRS) as h:
                            load_pair(h, False)
                            clear_slots(h)
                        sp.wait_ge(cl_ok, 16 * PAIRS)

                    @block.gpsimd
                    def _(g):
                        g.memset(zero[:, :], 0.0).then_inc(zr_ok, 1)
                        g.memset(cmask[:, :], 0.0).then_inc(mk, 1)
                        g.wait_ge(mk, 1)
                        lo = WIN_W // 2
                        for a in range(2):
                            part = cmask[a * GRID_W:(a + 1) * GRID_W, :]
                            g.affine_select(out=part[:, 0:GRID_W - WIN_W], in_=part[:, 0:GRID_W - WIN_W], compare_op=ALU.is_ge,
                                            fill=NEG, base=lo - (GRID_W - 1), pattern=[[1, GRID_W - WIN_W]],
                                            channel_multiplier=1).then_inc(mk, 1)
                            g.wait_ge(mk, 2 * a + 2)
                            g.affine_select(out=part[:, WIN_W:], in_=part[:, WIN_W:], compare_op=ALU.is_ge,
                                            fill=NEG, base=GRID_W - 1 + lo - 1 - WIN_W, pattern=[[-1, GRID_W - WIN_W]],
                                            channel_multiplier=-1).then_inc(mk, 1)
                            g.wait_ge(mk, 2 * a + 3)
                        cm = cmask[:, :]
                        cmb = bass.AP(tensor=cm.tensor, offset=cm.offset, ap=[list(cm.ap[0]), [0, NB], [1, GRID_W]])

                        def table(h, j, first):
                            g.wait_ge(rb_in[j], 32 * h + 32)
                            if not first:
                                g.wait_ge(neg_ok, UNITS * (h - 1) + NT * j + NTL)
                            link = Chain(g, pc, 2, 2 * h + j)
                            link(g.tensor_tensor(tab[j][:, 0:NB, :], raw[j][:, :, :], cmb, ALU.add))
                            g.sem_inc(g_passed, 1)
                            link(g.tensor_copy(tab[j][:, NB:NB + NI, :], tab[j][:, 2:2 + NI, :]))
                            g.sem_inc(g_passed, 1)
                            g.memset(tab[j][0:GRID_W, NB + 8:NB + 10, :], NEG).then_inc(mk, 1)
                            g.memset(tab[j][GRID_W:P, NB:NB + 1, :], NEG).then_inc(mk, 1)
                            g.memset(tab[j][GRID_W:P, NB + 9:NB + 10, :], NEG).then_inc(mk, 1)
                            g.wait_ge(mk, 5 + 3 * (2 * h + j) + 3)
                            g.sem_inc(bt_ok, 1)

                        for j in range(2):
                            table(0, j, True)
                        with g.Fori(1, PAIRS) as h:
                            for j in range(2):
                                table(h, j, False)

                    @block.scalar
                    def _(a):
                        a.sem_inc(ot_ok, 1)
                        a.wait_ge(b_in, 16)
                        a.activation(bq[:, 0, :], bq[:, 0, :], ACT.Copy, scale=HD ** -0.5).then_inc(b_ok, 1)
                        a.wait_ge(b_ok, 1)

                        def exps(h, u):
                            j, t, b = u // NT, u % NT, u % 2
                            nw, nk = keys(t)
                            a.wait_ge(neg_ok, UNITS * h + u + 1)
                            a.activation(prob[b][:, 0:nk], S[b][:, 0:nk], ACT.Exp, bias=small[:, b, 2:3],
                                         accum_out=sums[:, u:u + 1]).then_inc(exp_ok, 1)

                        def oT(h):
                            a.wait_ge(to_ok, h + 1)
                            bias = bq[:, 2, bass.ds(h, 1)]
                            dst = OT[:, bass.ds(h, 1), :].rearrange("p o n -> p (o n)")
                            a.activation(dst[:, 0:L].rearrange("p (r c) -> p r c", c=GRID_W), rows_reversed(QK[1][:, 0:L], ROWS),
                                         ACT.Identity, bias=bias).then_inc(ot_ok, 1)
                            a.activation(dst[:, L:N], QK[1][:, L:N], ACT.Identity, bias=bias).then_inc(ot_ok, 1)

                        with a.Fori(0, PAIRS) as h:
                            a.wait_ge(qkv_ps, 3 * h + 1)
                            bias = bq[:, 0, bass.ds(h, 1)]
                            src = QK[0][:, 0:L].rearrange("p (r c) -> p r c", c=GRID_W)
                            a.activation(rows_reversed(qT[:, 0:L], ROWS), src, ACT.Identity, bias=bias, scale=HD ** -0.5).then_inc(q_ok, 1)
                            a.activation(qT[:, L:N], QK[0][:, L:N], ACT.Identity, bias=bias, scale=HD ** -0.5).then_inc(q_ok, 1)
                            a.wait_ge(qkv_ps, 3 * h + 3)
                            a.activation(flat(V[:, :, :]), QK[0][:, 0:N], ACT.Copy).then_inc(v_ok, 1)
                            exps(h, 0)
                            exps(h, 1)
                            for u in range(UNITS):
                                b = u % 2
                                nk = keys(u % NT)[1]
                                half = nk // P // 2 * P
                                a.wait_ge(pt_ok, UNITS * h + u + 1)
                                a.activation(probT[b][:, 0:half], PT[:, 0:half], ACT.Copy).then_inc(pa_ok, 1)
                                if u + 2 < UNITS:
                                    exps(h, u + 2)
                            oT(h)

                    @block.vector
                    def _(v):
                        v.wait_ge(b_in, 16)

                        def softmax(h, u, link):
                            j, t, b = u // NT, u % NT, u % 2
                            nw, nk = keys(t)
                            v.wait_ge(s_ok, UNITS * h + u + 1)
                            link(v.reduce_max(small[:, b, 0:1], S[b][:, nw:nk], AX))
                            mx = small[:, b, 0:1]
                            if nw:
                                if u % NT == 0:
                                    v.wait_ge(bt_ok, 2 * h + j + 1)
                                r0 = window(t)[2]
                                v.sem_inc(v_passed, 1)
                                link(v.tensor_tensor_reduce(S[b][:, 0:nw], S[b][:, 0:nw], flat(tab[j][:, r0:r0 + nw // GRID_W, :]),
                                                            1.0, mx, ALU.add, ALU.max, small[:, b, 1:2]))
                                mx = small[:, b, 1:2]
                            v.tensor_scalar(small[:, b, 2:3], mx, -1.0, None, ALU.mult).then_inc(neg_ok, 1)

                        with v.Fori(0, PAIRS) as h:
                            v.wait_ge(qkv_ps, 3 * h + 2)
                            v.tensor_scalar(kT[:, :], QK[1][:, 0:N], bq[:, 1, bass.ds(h, 1)], None, ALU.add).then_inc(k_ok, 1)
                            link = Chain(v, dv, 2 * (2 * NTL + NTC) + UNITS, h)
                            softmax(h, 0, link)
                            softmax(h, 1, link)
                            for u in range(UNITS):
                                j, t, b = u // NT, u % NT, u % 2
                                nk = keys(t)[1]
                                half = nk // P // 2 * P
                                v.wait_ge(pt_ok, UNITS * h + u + 1)
                                v.tensor_copy(probT[b][:, half:nk], PT[:, 512:512 + nk - half]).then_inc(pd_ok, 1)
                                if u + 2 < UNITS:
                                    softmax(h, u + 2, link)
                                v.wait_ge(o_ok, UNITS * h + u + 1)
                                v.wait_ge(exp_ok, UNITS * h + u + 1)
                                link(v.reciprocal(small[:, b, 3:4], sums[:, u:u + 1]))
                                v.tensor_scalar(osb[:, t, j * HD:(j + 1) * HD], PS[:, 6 + b, 0:HD],
                                                small[:, b, 3:4], None, ALU.mult).then_inc(on_ok, 1)
                            link.end()

                    @block.tensor
                    def _(t_):
                        pe = t_

                        def scores(h, u):
                            j, t, b = u // NT, u % NT, u % 2
                            nw, nk = keys(t)
                            q = qT[j * HD:(j + 1) * HD, t * P:(t + 1) * P]
                            k = kT[j * HD:(j + 1) * HD, :]
                            if nw:
                                k0 = window(t)[0] * GRID_W
                                pe.matmul(S[b][:, 0:512], q, k[:, k0:k0 + 512], start=True, stop=True)
                                if nw > 512:
                                    pe.matmul(S[b][:, 512:nw], q, k[:, k0 + 512:k0 + nw], start=True, stop=True)
                            pe.matmul(S[b][:, nw:nk], q, k[:, L:N], start=True, stop=True).then_inc(s_ok, 1)

                        with pe.Fori(0, PAIRS) as h:
                            for m in range(2):
                                pe.wait_ge(sl_in[m], 16 * h + 16)
                                if m == 1:
                                    pe.wait_ge(ot_ok, 2 * h + 1)
                                for c, w in ((0, 512), (512, 512), (1024, 256)):
                                    for k in range(KD):
                                        mm = pe.matmul(QK[m][:, c:c + w], slab[m][:, k, :], hT[:, k, c:c + w],
                                                       start=(k == 0), stop=(k == KD - 1))
                                mm.then_inc(qkv_ps, 1)
                            pe.wait_ge(sl_in[2], 16 * h + 16)
                            pe.wait_ge(q_ok, 2 * h + 2)
                            for t in range(NT):
                                for k in range(KD):
                                    mm = pe.matmul(QK[0][:, t * P:(t + 1) * P], hT[:, k, t * P:(t + 1) * P], slab[2][:, k, :],
                                                   start=(k == 0), stop=(k == KD - 1))
                            mm.then_inc(qkv_ps, 1)
                            pe.wait_ge(v_ok, h + 1)
                            pe.wait_ge(k_ok, h + 1)
                            scores(h, 0)
                            scores(h, 1)
                            for u in range(UNITS):
                                j, t, b = u // NT, u % NT, u % 2
                                nw, nk = keys(t)
                                nc_ = nk // P
                                pe.wait_ge(exp_ok, UNITS * h + u + 1)
                                for c in range(nc_):
                                    at = c * P if c < nc_ // 2 else 512 + (c - nc_ // 2) * P
                                    mm = pe.transpose(PT[:, at:at + P], prob[b][:, c * P:(c + 1) * P], ident[:, :])
                                mm.then_inc(pt_ok, 1)
                                if u + 2 < UNITS:
                                    scores(h, u + 2)
                                pe.wait_ge(pa_ok, UNITS * h + u + 1)
                                pe.wait_ge(pd_ok, UNITS * h + u + 1)
                                if u >= 2:
                                    pe.wait_ge(on_ok, UNITS * h + u - 1)
                                tiles = [window(t)[0] // 2 + c for c in range(nw // P)] + [NTL, NTL + 1]
                                for c, kt in enumerate(tiles):
                                    mm = pe.matmul(PS[:, 6 + b, 0:HD], probT[b][:, c * P:(c + 1) * P],
                                                   V[:, kt, j * HD:(j + 1) * HD], start=(c == 0), stop=(c == nc_ - 1))
                                mm.then_inc(o_ok, 1)
                            pe.wait_ge(on_ok, UNITS * h + UNITS)
                            for t in range(NT):
                                mm = pe.transpose(QK[1][:, t * P:(t + 1) * P], osb[:, t, :], ident[:, :])
                            mm.then_inc(to_ok, 1)

        def projection(l, nt, Z, w_o, b_o, RL):
            n_pairs = nt // 2
            with ExitStack() as st:
                wo = sbuf(st, f"wo{l}", [P, KD, D])
                wr = sbuf(st, f"wr{l}", [P, KD, NR])
                rbias = sbuf(st, f"rbias{l}", [P, NR])
                ng, bo = sbuf(st, f"ng_p{l}", [P, D]), sbuf(st, f"bo{l}", [P, D])
                bg = sbuf(st, f"bg{l}", [P, 2, D])
                xt = [sbuf(st, f"xt_p{l}{j}", [P, D]) for j in range(2)]
                x1 = [sbuf(st, f"x1_p{l}{j}", [P, D]) for j in range(2)]
                hb = [sbuf(st, f"hb_p{l}{j}", [P, D]) for j in range(2)]
                ht = [sbuf(st, f"ht_p{l}{j}", [P, KD, P]) for j in range(2)]
                junk = sbuf(st, f"junk_p{l}", [P, D])
                ss, rt = sbuf(st, f"ss_p{l}", [P, 2]), sbuf(st, f"rt_p{l}", [P, 2])
                nm = lambda s: sem(f"{s}_p{l}")
                wo_in, wr_in, rows_in, rows_ok, bg_ok = nm("wo_in"), nm("wr_in"), nm("rows"), nm("gain"), nm("bg")
                x_in = [nm(f"x_in{j}") for j in range(2)]
                x_out = [nm(f"x1_out{j}") for j in range(2)]
                h_out = [nm(f"h_out{j}") for j in range(2)]
                xb_ok, op_ok, x1_ok, sum_ok, sqrt_ok, h_ok = nm("xb"), nm("op"), nm("x1"), nm("sum"), nm("sqrt"), nm("h")
                tr_ok, ev_ok, rt_ok, rl_ok, dv = nm("tr"), nm("ev"), nm("router"), nm("rl"), nm("dve")

                with nc.Block() as block:
                    @block.sync
                    def _(sp):
                        load_rows(sp, rows_in, l, 1, A["norm_g"][l, 1, :], ng[:, :])
                        load_gate(sp, rows_in, l, 0)
                        sp.dma_start(bo[:, :], row_to_all(b_o, D)).then_inc(rows_in, 16)

                        def load_x(j, src):
                            sp.dma_start(xt[j][:, :], src).then_inc(x_in[j], 16)

                        def source(n, i, j):
                            if l:
                                return x2_d[bass.ds((2 * i + j) * P, P), :]
                            return A["x"][0, bass.ds((2 * i + j) * P, P), :]

                        for j in range(2):
                            load_x(j, x2_d[j * P:(j + 1) * P, :] if l else A["x"][0, j * P:(j + 1) * P, :])
                        sp.dma_start(wo[:, :, :], w_o.rearrange("(k p) n -> p k n", p=P)).then_inc(wo_in, 16)
                        sp.dma_start(rbias[:, 0:GROUPS], row_to_all(A["moe_b_group"][l, :], GROUPS)).then_inc(wr_in, 16)
                        sp.dma_start(rbias[:, GROUPS:NR], row_to_all(A["moe_b_expert"][l, 0, :], EXPERTS)).then_inc(wr_in, 16)
                        sp.dma_start(wr[:, :, 0:GROUPS], A["moe_w_group"][l].rearrange("(k p) g -> p k g", p=P)).then_inc(wr_in, 16)
                        for g in range(GROUPS):
                            sp.dma_start(wr[:, :, GROUPS + g * EPG:GROUPS + (g + 1) * EPG],
                                         A["moe_w_expert"][l, g].rearrange("(k p) e -> p k e", p=P)).then_inc(wr_in, 16)
                        with sp.Fori(1, NTL // 2) as i:
                            for j in range(2):
                                sp.wait_ge(x1_ok, 2 * i + j - 1)
                                load_x(j, source(None, i, j))
                        if nt > NTL:
                            for j in range(2):
                                sp.wait_ge(x1_ok, NTL + j - 1)
                                load_x(j, A["ctx"][0, j * P:(j + 1) * P, :])

                    @block.gpsimd
                    def _(g):
                        def bias(n, j, w):
                            g.wait_ge(x_in[j], (n - j) * 8 + 16)
                            g.tensor_tensor(xt[j][:, :], xt[j][:, :], bg[:, w, :], ALU.add).then_inc(xb_ok, 1)

                        g.wait_ge(bg_ok, 2)
                        with g.Fori(0, NTL // 2) as i:
                            for j in range(2):
                                bias(2 * i + j, j, 0)
                        if nt > NTL:
                            bias(NTL, 0, 1)
                            bias(NTL + 1, 1, 1)

                    @block.vector
                    def _(v):
                        v.wait_ge(rows_in, 128)
                        gain(v, ng[:, :], rows_ok)
                        for w in range(2):
                            v.tensor_tensor(bg[:, w, :], gt_rows[:, w, :], bo[:, :], ALU.mult).then_inc(bg_ok, 1)
                        v.wait_ge(bg_ok, 2)
                        v.wait_ge(wr_in, 16 * 7)

                        def tile(n, j, w, first=False):
                            link = Chain(v, dv, 4, n)
                            v.wait_ge(op_ok, n + 1)
                            if not first:
                                v.wait_ge(x_out[j], (n - j) * 8)
                            link(v.tensor_tensor(x1[j][:, :], banks(2 * j, 2), gt_rows[:, w, :], ALU.mult))
                            v.wait_ge(xb_ok, n + 1)
                            v.tensor_tensor(x1[j][:, :], x1[j][:, :], xt[j][:, :], ALU.add).then_inc(x1_ok, 1)
                            v.wait_ge(x1_ok, n + 1)
                            link(v.tensor_tensor_reduce(junk[:, :], x1[j][:, :], x1[j][:, :], 1.0 / D, 0.0, ALU.mult, ALU.add,
                                                        ss[:, j:j + 1]))
                            v.sem_inc(sum_ok, 1)
                            v.wait_ge(sqrt_ok, n + 1)
                            link(v.reciprocal(ss[:, j:j + 1], rt[:, j:j + 1]))
                            if not first:
                                v.wait_ge(tr_ok, n - 1)
                                v.wait_ge(h_out[j], (n - j) * 8)
                            link(v.scalar_tensor_tensor(out=hb[j][:, :], in0=x1[j][:, :], scalar=ss[:, j:j + 1],
                                                        in1=g_rows[:, w, :], op0=ALU.mult, op1=ALU.mult))
                            v.tensor_tensor(hb[j][:, :], hb[j][:, :], sh_rows[:, w, :], ALU.add).then_inc(h_ok, 1)
                            link.end()

                        def logits(n):
                            v.wait_ge(rt_ok, n + 1)
                            dst = RL[:, bass.ds(n, 1), :].rearrange("p o n -> p (o n)")
                            v.tensor_tensor(dst, PS[:, 6, 0:NR], rbias[:, :], ALU.add).then_inc(rl_ok, 1)

                        tile(0, 0, 0, True)
                        tile(1, 1, 0, True)
                        logits(0)
                        with v.Fori(1, NTL // 2) as i:
                            tile(2 * i, 0, 0)
                            logits(2 * i - 1)
                            tile(2 * i + 1, 1, 0)
                            logits(2 * i)
                        for n in range(NTL, nt):
                            tile(n, n % 2, 1)
                            logits(n - 1)
                        logits(nt - 1)

                    @block.scalar
                    def _(a):
                        def tile(n, j, rows, first=False):
                            a.wait_ge(x1_ok, n + 1)
                            a.dma_start(x1_d[rows, :], x1[j][:, :]).then_inc(x_out[j], 16)
                            a.wait_ge(sum_ok, n + 1)
                            if not first:
                                a.wait_ge(dv, 4 * (n - 2) + 3)
                            a.activation(rt[:, j:j + 1], ss[:, j:j + 1], ACT.Sqrt, bias=epst[:, :]).then_inc(sqrt_ok, 1)
                            a.wait_ge(h_ok, n + 1)
                            a.dma_start(h2_d[rows, :], hb[j][:, :]).then_inc(h_out[j], 16)

                        def evac(n, j):
                            a.wait_ge(tr_ok, n + 1)
                            a.wait_ge(rt_ok, n - 1) if not isinstance(n, int) or n >= 2 else None
                            a.activation(flat(ht[j][:, :, :]), banks(4, 2), ACT.Copy).then_inc(ev_ok, 1)

                        tile(0, 0, slice(0, P), True)
                        evac(0, 0)
                        tile(1, 1, slice(P, 2 * P), True)
                        evac(1, 1)
                        with a.Fori(1, nt // 2) as i:
                            for j in range(2):
                                tile(2 * i + j, j, bass.ds((2 * i + j) * P, P))
                                evac(2 * i + j, j)
                        for j in range(2):
                            a.wait_ge(x_out[j], 8 * nt)
                            a.wait_ge(h_out[j], 8 * nt)

                    @block.tensor
                    def _(t):
                        def product(n):
                            if n >= 2:
                                t.wait_ge(x1_ok, n - 1)
                            for h in range(2):
                                for k in range(KD):
                                    mm = t.matmul(PS[:, 2 * (n % 2) + h, :], Z[:, k, n * P:(n + 1) * P],
                                                  wo[:, k, h * 512:(h + 1) * 512], start=(k == 0), stop=(k == KD - 1))
                            mm.then_inc(op_ok, 1)

                        def route(n):
                            t.wait_ge(ev_ok, n + 1)
                            if n >= 1:
                                t.wait_ge(rl_ok, n)
                            for k in range(KD):
                                mm = t.matmul(PS[:, 6, 0:NR], ht[n % 2][:, k, :], wr[:, k, :], start=(k == 0), stop=(k == KD - 1))
                            mm.then_inc(rt_ok, 1)

                        t.wait_ge(wo_in, 16)
                        t.wait_ge(wr_in, 16 * 7)
                        product(0)
                        for n in range(nt):
                            if n + 1 < nt:
                                product(n + 1)
                            if n:
                                route(n - 1)
                            transposes(t, n, n % 2, hb, h_ok, 4, ev_ok, tr_ok)
                        route(nt - 1)

        def routing(l, nt, RL, tabs):
            dst, w01, item, item_slots, n_pairs = tabs
            with ExitStack() as st:
                T = lambda name, shape, dt=F32: sbuf(st, f"{name}_r{l}", [P] + shape, dt)
                io8i, ioti, toki, zi = T("io8i", [EPG], I32), T("ioti", [ITEMS], I32), T("toki", [NT], I32), T("zi", [ITEMS], I32)
                io8, iot = T("io8", [EPG]), T("iot", [ITEMS])
                gl, el, m4 = T("gl", [nt, GROUPS]), T("el", [nt, GROUPS, EPG]), T("m4", [nt, GROUPS])
                e8, m8, oh0, oh1 = T("e8", [nt, EPG]), T("m8", [nt, EPG]), T("oh0", [nt, EPG]), T("oh1", [nt, EPG])
                gmax, gsum, best, v0, v1 = (T(x, [nt]) for x in ("gmax", "gsum", "best", "v0", "v1"))
                goh = T("goh", [nt, GROUPS])
                OH = [T(f"OH{k}", [nt, EXPERTS]) for k in range(2)]
                A2, pre, cnt, run = T("A2", [nt, EXPERTS]), T("pre", [nt, EXPERTS]), T("cnt", [nt, EXPERTS]), T("run", [EXPERTS])
                blk, incl, base, one32 = T("blk", [EXPERTS]), T("incl", [EXPERTS]), T("base", [EXPERTS]), T("one32", [EXPERTS])
                NBLK = nt + 1
                cmpb, cmpi = T("cmpb", [EXPERTS, NBLK]), T("cmpi", [ITEMS, EXPERTS])
                itf, npf, cmpn = T("itf", [ITEMS]), T("npf", [1]), T("cmpn", [ITEMS // 2])
                df, dq, hi, adr = T("df", [2, nt]), T("dq", [2, nt]), T("hi", [2, nt]), T("adr", [2, nt], I32)
                cmph = T("cmph", [2 * nt, ITEMS - 1])
                prod = T("prod", [nt, EXPERTS])
                nm = lambda s: sem(f"{s}_r{l}")
                io_ok, dv, d_ok, e_ok, a_ok, cn_ok = nm("iota"), nm("dve"), nm("diff"), nm("exp"), nm("assigned"), nm("counts")
                z_ok, ad_ok, sc_ok, sl_ok = nm("zeroed"), nm("slots"), gather_sem(f"scattered_r{l}"), nm("loaded")
                with nc.Block() as block:
                    @block.gpsimd
                    def _(g):
                        g.memset(zi[:, :], 0).then_inc(io_ok, 1)
                        g.iota(io8i[:, :], pattern=[[-1, EPG]], base=EPG, channel_multiplier=0).then_inc(io_ok, 1)
                        g.iota(ioti[:, :], pattern=[[1, ITEMS]], base=0, channel_multiplier=0).then_inc(io_ok, 1)
                        g.iota(toki[:, :], pattern=[[P, NT]], base=0, channel_multiplier=1).then_inc(io_ok, 1)
                        g.wait_ge(io_ok, 4)
                        g.wait_ge(z_ok, 16)
                        g.wait_ge(ad_ok, 1)
                        for k in range(2):
                            for t in range(nt):
                                g.indirect_dma_start(out=slot_d[l][:, :], in_=toki[:, t:t + 1], in_offset=None,
                                                     out_offset=bass.IndirectOffsetOnAxis(ap=adr[:, k, t:t + 1], axis=0)
                                                     ).then_inc(sc_ok, 16)

                    @block.sync
                    def _(sp):
                        sp.wait_ge(io_ok, 4)
                        sp.dma_start(slot_d[l].rearrange("(p i) o -> p (i o)", p=P), zi[:, :]).then_inc(z_ok, 16)
                        sp.wait_ge(sc_ok, 2 * nt * 16)
                        sp.dma_start(item_slots[:, :], slot_d[l].rearrange("(p i) o -> p (i o)", p=P)).then_inc(sl_ok, 16)
                        sp.wait_ge(sl_ok, 16)

                    @block.scalar
                    def _(a):
                        a.wait_ge(d_ok, 1)
                        a.activation(flat(m4[:, :, :]), flat(gl[:, :, :]), ACT.Exp).then_inc(e_ok, 1)
                        a.wait_ge(d_ok, 2)
                        a.activation(v1[:, :], v1[:, :], ACT.Exp).then_inc(e_ok, 1)

                    @block.tensor
                    def _(t):
                        t.wait_ge(a_ok, 1)
                        t.matmul(PS[:, 0, 0:nt * EXPERTS], ltri[:, :], flat(A2[:, :, :]), start=True, stop=True)
                        t.matmul(PS[:, 1, 0:nt * EXPERTS], ones[:, :], flat(A2[:, :, :]), start=True, stop=True).then_inc(cn_ok, 1)

                    @block.vector
                    def _(v):
                        n = [0]

                        def link(ins):
                            n[0] += 1
                            ins.then_inc(dv, 1)
                            v.wait_ge(dv, n[0])

                        def first_best(val, mx, mask, hot, width):
                            link(v.tensor_reduce(mx[:, :], val[:, :, :], AX, ALU.max))
                            link(v.tensor_tensor(mask[:, :, :], val[:, :, :], expand(mx[:, :], (2, width)), ALU.is_equal))
                            link(v.tensor_tensor(mask[:, :, :], mask[:, :, :], expand(io8[:, 0:width], (1, nt)), ALU.mult))
                            link(v.tensor_reduce(best[:, :], mask[:, :, :], AX, ALU.max))
                            link(v.tensor_tensor(hot[:, :, :], mask[:, :, :], expand(best[:, :], (2, width)), ALU.is_equal))

                        v.wait_ge(io_ok, 4)
                        link(v.tensor_copy(io8[:, :], io8i[:, :]))
                        link(v.tensor_copy(iot[:, :], ioti[:, :]))
                        link(v.memset(one32[:, :], 1.0))
                        link(v.tensor_copy(gl[:, :, :], RL[:, 0:nt, 0:GROUPS]))
                        first_best(gl, gmax, m4, goh, GROUPS)
                        v.tensor_tensor(gl[:, :, :], gl[:, :, :], expand(gmax[:, :], (2, GROUPS)), ALU.subtract).then_inc(d_ok, 1)
                        rle = RL[:, 0:nt, GROUPS:NR].rearrange("p t (g e) -> p t g e", g=GROUPS)
                        link(v.tensor_tensor(el[:, :, :, :], rle, expand(goh[:, :, :], (3, EPG)), ALU.mult))
                        link(v.tensor_reduce(e8[:, :, :], el[:, :, :, :].rearrange("p t g e -> p t e g"), AX, ALU.add))
                        first_best(e8, v0, m8, oh0, EPG)
                        link(v.tensor_scalar(m8[:, :, :], oh0[:, :, :], NEG, None, ALU.mult))
                        link(v.tensor_tensor(e8[:, :, :], e8[:, :, :], m8[:, :, :], ALU.add))
                        first_best(e8, v1, m8, oh1, EPG)
                        v.tensor_tensor(v1[:, :], v1[:, :], v0[:, :], ALU.subtract).then_inc(d_ok, 1)
                        v.wait_ge(e_ok, 2)
                        link(v.tensor_reduce(gsum[:, :], m4[:, :, :], AX, ALU.add))
                        link(v.tensor_scalar(v0[:, :], v1[:, :], 1.0, None, ALU.add))
                        link(v.tensor_tensor(v0[:, :], v0[:, :], gsum[:, :], ALU.mult))
                        link(v.reciprocal(w01[:, 0, :], v0[:, :]))
                        link(v.tensor_tensor(w01[:, 1, :], w01[:, 0, :], v1[:, :], ALU.mult))
                        for k, oh in enumerate((oh0, oh1)):
                            link(v.tensor_tensor(OH[k][:, :, :].rearrange("p t (g e) -> p t g e", g=GROUPS),
                                                 expand(goh[:, :, :], (3, EPG)), expand(oh[:, :, :], (2, GROUPS)), ALU.mult))
                        v.tensor_tensor(A2[:, :, :], OH[0][:, :, :], OH[1][:, :, :], ALU.add).then_inc(a_ok, 1)
                        v.wait_ge(cn_ok, 1)
                        link(v.tensor_copy(flat(pre[:, :, :]), PS[:, 0, 0:nt * EXPERTS]))
                        link(v.tensor_copy(flat(cnt[:, :, :]), PS[:, 1, 0:nt * EXPERTS]))
                        link(v.tensor_copy(run[:, :], cnt[:, 0, :]))
                        for t in range(1, nt):
                            link(v.tensor_tensor(pre[:, t, :], pre[:, t, :], run[:, :], ALU.add))
                            link(v.tensor_tensor(run[:, :], run[:, :], cnt[:, t, :], ALU.add))
                        link(v.tensor_scalar(run[:, :], run[:, :], 1.0 / P, None, ALU.mult))
                        link(v.tensor_tensor(cmpb[:, :, :], expand(run[:, :], (2, NBLK)), expand(iot[:, 0:NBLK], (1, EXPERTS)), ALU.is_gt))
                        link(v.tensor_reduce(blk[:, :], cmpb[:, :, :], AX, ALU.add))
                        link(v.tensor_tensor_scan(incl[:, :], one32[:, :], blk[:, :], 0.0, ALU.mult, ALU.add))
                        link(v.tensor_tensor(base[:, :], incl[:, :], blk[:, :], ALU.subtract))
                        link(v.tensor_scalar(base[:, :], base[:, :], float(P), None, ALU.mult))
                        link(v.tensor_tensor(pre[:, :, :], pre[:, :, :], expand(base[:, :], (1, nt)), ALU.add))
                        for k in range(2):
                            link(v.tensor_tensor(prod[:, :, :], pre[:, :, :], OH[k][:, :, :], ALU.mult))
                            link(v.tensor_reduce(df[:, k, :], prod[:, :, :], AX, ALU.add))
                        link(v.tensor_copy(flat(dst[:, :, :]), flat(df[:, :, :])))
                        link(v.tensor_scalar(flat(dq[:, :, :]), flat(df[:, :, :]), 1.0 / P, None, ALU.mult))
                        link(v.tensor_tensor(cmph[:, :, :], expand(flat(dq[:, :, :]), (2, ITEMS - 1)),
                                             expand(iot[:, 1:ITEMS], (1, 2 * nt)), ALU.is_ge))
                        link(v.tensor_reduce(flat(hi[:, :, :]), cmph[:, :, :], AX, ALU.add))
                        link(v.tensor_scalar(flat(hi[:, :, :]), flat(hi[:, :, :]), -(P * ITEMS - 1.0), None, ALU.mult))
                        link(v.scalar_tensor_tensor(out=flat(hi[:, :, :]), in0=flat(df[:, :, :]), scalar=float(ITEMS),
                                                    in1=flat(hi[:, :, :]), op0=ALU.mult, op1=ALU.add))
                        v.tensor_copy(flat(adr[:, :, :]), flat(hi[:, :, :])).then_inc(ad_ok, 1)
                        link(v.tensor_tensor(cmpi[:, :, :], expand(iot[:, :], (2, EXPERTS)), expand(incl[:, :], (1, ITEMS)), ALU.is_ge))
                        link(v.tensor_reduce(itf[:, :], cmpi[:, :, :], AX, ALU.add))
                        link(v.tensor_scalar(itf[:, :], itf[:, :], EXPERTS - 1.0, None, ALU.min))
                        link(v.tensor_copy(item[:, :], itf[:, :]))
                        link(v.tensor_scalar(cmpn[:, :], iot[:, 0:ITEMS:2], incl[:, EXPERTS - 1:EXPERTS], None, ALU.is_lt))
                        link(v.tensor_reduce(npf[:, :], cmpn[:, :], AX, ALU.add))
                        link(v.tensor_copy(n_pairs[:, :], npf[:, :]))

        def experts(l, tabs):
            dst, w01, item, item_slots, n_pairs = tabs
            with ExitStack() as st:
                W1 = [sbuf(st, f"w1_{l}{j}", [P, KD, FF]) for j in range(2)]
                W3 = [sbuf(st, f"w3_{l}{j}", [P, KD, FF]) for j in range(2)]
                W2 = [sbuf(st, f"w2_{l}{j}", [P, KF, D]) for j in range(2)]
                ib = [sbuf(st, f"ib_{l}{j}", [P, 1], I32) for j in range(2)]
                xg = [sbuf(st, f"xg_{l}{j}", [P, D]) for j in range(2)]
                xT = [sbuf(st, f"xT_{l}{j}", [P, KD, P]) for j in range(2)]
                th, hid = sbuf(st, f"th_{l}", [P, FF]), sbuf(st, f"hid_{l}", [P, FF])
                hT_ = sbuf(st, f"hidT_{l}", [P, KF, P])
                y = [sbuf(st, f"y_{l}{j}", [P, D]) for j in range(2)]
                nm = lambda s: sem(f"{s}_e{l}")
                w1_in, w3_in, w2_in, y_out = ([nm(f"{x}{j}") for j in range(2)] for x in ("w1", "w3", "w2", "y_out"))
                g_in = [gather_sem(f"rows{j}_e{l}") for j in range(2)]
                ib_ok, xt_ps, xt_ok, up_ok, th_ok, u_ok, hid_ok = (nm(x) for x in ("ib", "xT_ps", "xT", "up", "tanh", "u", "hid"))
                ht_ps, ht_ok, y_ps, ya_ok, yd_ok = (nm(x) for x in ("hidT_ps", "hidT", "y_ps", "y_act", "y_dve"))
                passed, a_passed = nm("passed"), nm("act_passed")
                w1v, w3v = (A[k][l].rearrange("e (k p) f -> e p k f", p=P) for k in ("moe_w1", "moe_w3"))
                w2v = A["moe_w2"][l].rearrange("e (k p) d -> e p k d", p=P)

                with nc.Block() as block:
                    @block.sync
                    def _(sp):
                        count = sp.value_load(n_pairs[0:1, 0:1], min_val=1, max_val=(MAX_ITEMS + 1) // 2)
                        with sp.Fori(0, count) as i:
                            for j in range(2):
                                n = 2 * i + j
                                e = sp.value_load(item[0:1, bass.ds(n, 1)], min_val=0, max_val=EXPERTS - 1)
                                sp.wait_ge(up_ok, n + 1)
                                sp.dma_start(W1[j][:, :, :], w1v[bass.ds(e, 1)].rearrange("o p k f -> (o p) k f")).then_inc(w1_in[j], 16)
                                sp.dma_start(W3[j][:, :, :], w3v[bass.ds(e, 1)].rearrange("o p k f -> (o p) k f")).then_inc(w3_in[j], 16)
                                sp.wait_ge(y_ps, n + 1)
                                sp.dma_start(W2[j][:, :, :], w2v[bass.ds(e, 1)].rearrange("o p k d -> (o p) k d")).then_inc(w2_in[j], 16)

                    @block.gpsimd
                    def _(g):
                        count = g.value_load(n_pairs[0:1, 0:1], min_val=1, max_val=(MAX_ITEMS + 1) // 2)

                        def gather(n, j):
                            g.wait_ge(xt_ps, n + 1)
                            g.tensor_copy(ib[j][:, :], item_slots[:, bass.ds(n, 1)]).then_inc(ib_ok, 1)
                            g.wait_ge(ib_ok, n + 1)
                            g.sem_inc(passed, 1)
                            g.indirect_dma_start(out=xg[j][:, :], out_offset=None, in_=h2_d[:, :],
                                                 in_offset=bass.IndirectOffsetOnAxis(ap=ib[j][:, :], axis=0)).then_inc(g_in[j], 16)

                        gather(0, 0)
                        with g.Fori(0, count) as i:
                            gather(2 * i + 1, 1)
                            gather(2 * i + 2, 0)
                        g.wait_ge(g_in[0], count * 16 + 16)

                    @block.scalar
                    def _(a):
                        count = a.value_load(n_pairs[0:1, 0:1], min_val=1, max_val=(MAX_ITEMS + 1) // 2)

                        def rows_T(n, j):
                            a.wait_ge(xt_ps, n + 3)
                            a.activation(flat(xT[j][:, :, :]), banks(0, 2), ACT.Copy).then_inc(xt_ok, 1)

                        for s in (xt_ok, ya_ok):
                            a.sem_inc(s, 1)
                        for j in range(2):
                            a.sem_inc(y_out[j], 16)
                        rows_T(0, 0)
                        with a.Fori(0, count) as i:
                            for j in range(2):
                                n = 2 * i + j
                                a.wait_ge(up_ok, n + 3)
                                a.activation(th[:, :], PS[:, 2, :], ACT.Tanh, scale=0.5).then_inc(th_ok, 1)
                                rows_T(n + 1, 1 - j)
                                a.wait_ge(y_ps, n + 3)
                                a.wait_ge(y_out[j], 16 * i + 16)
                                a.activation(y[j][:, 0:512], PS[:, 5, :], ACT.Copy).then_inc(ya_ok, 1)
                                a.wait_ge(ya_ok, n + 2)
                                a.wait_ge(yd_ok, n + 2)
                                a.dma_start(ys_d[bass.ds(n * P, P), :], y[j][:, :]).then_inc(y_out[j], 16)
                        for j in range(2):
                            a.wait_ge(y_out[j], 16 * count + 16)
                        a.sem_inc(a_passed, 1)

                    @block.vector
                    def _(v):
                        count = v.value_load(n_pairs[0:1, 0:1], min_val=1, max_val=(MAX_ITEMS + 1) // 2)
                        v.sem_inc(yd_ok, 1)
                        with v.Fori(0, count) as i:
                            for j in range(2):
                                n = 2 * i + j
                                v.wait_ge(th_ok, n + 1)
                                v.scalar_tensor_tensor(out=th[:, :], in0=th[:, :], scalar=1.0, in1=PS[:, 2, :],
                                                       op0=ALU.add, op1=ALU.mult).then_inc(u_ok, 1)
                                v.wait_ge(u_ok, n + 1)
                                v.scalar_tensor_tensor(out=hid[:, :], in0=th[:, :], scalar=0.5, in1=PS[:, 3, :],
                                                       op0=ALU.mult, op1=ALU.mult).then_inc(hid_ok, 1)
                                v.wait_ge(ht_ps, n + 1)
                                v.tensor_copy(flat(hT_[:, :, :]), PS[:, 4, :]).then_inc(ht_ok, 1)
                                v.wait_ge(y_ps, n + 3)
                                v.wait_ge(y_out[j], 16 * i + 16)
                                v.tensor_copy(y[j][:, 512:D], PS[:, 6, :]).then_inc(yd_ok, 1)

                    @block.tensor
                    def _(t):
                        count = t.value_load(n_pairs[0:1, 0:1], min_val=1, max_val=(MAX_ITEMS + 1) // 2)
                        t.sem_inc(up_ok, 2)
                        t.sem_inc(y_ps, 2)
                        t.sem_inc(xt_ps, 2)

                        def rows_T(n, j, half):
                            t.wait_ge(g_in[j], half * 16 + 16)
                            t.wait_ge(xt_ok, n + 1)
                            for k in range(KD):
                                mm = t.transpose(banks(0, 2)[:, k * P:(k + 1) * P], xg[j][:, k * P:(k + 1) * P], ident[:, :])
                            mm.then_inc(xt_ps, 1)

                        rows_T(0, 0, 0)
                        with t.Fori(0, count) as i:
                            for j in range(2):
                                n = 2 * i + j
                                t.wait_ge(xt_ok, n + 2)
                                for W, s, bank in ((W1, w1_in, 2), (W3, w3_in, 3)):
                                    t.wait_ge(s[j], 16 * i + 16)
                                    for k in range(KD):
                                        mm = t.matmul(PS[:, bank, :], xT[j][:, k, :], W[j][:, k, :], start=(k == 0), stop=(k == KD - 1))
                                mm.then_inc(up_ok, 1)
                                rows_T(n + 1, 1 - j, i + j)
                                t.wait_ge(hid_ok, n + 1)
                                for k in range(KF):
                                    mm = t.transpose(PS[:, 4, k * P:(k + 1) * P], hid[:, k * P:(k + 1) * P], ident[:, :])
                                mm.then_inc(ht_ps, 1)
                                t.wait_ge(w2_in[j], 16 * i + 16)
                                t.wait_ge(ht_ok, n + 1)
                                t.wait_ge(ya_ok, n + 1)
                                t.wait_ge(yd_ok, n + 1)
                                for h in range(2):
                                    for k in range(KF):
                                        mm = t.matmul(PS[:, 5 + h, :], hT_[:, k, :], W2[j][:, k, h * 512:(h + 1) * 512],
                                                      start=(k == 0), stop=(k == KF - 1))
                                mm.then_inc(y_ps, 1)

        def combine(l, nt, tabs, hT):
            dst, w01 = tabs[0], tabs[1]
            last = hT is None
            with ExitStack() as st:
                ng = sbuf(st, f"ng_c{l}", [P, D])
                bufs = lambda name, shape, dt=F32: [sbuf(st, f"{name}_c{l}{j}", shape, dt) for j in range(2)]
                ib, wb = bufs("ib", [P, 2], I32), bufs("wb", [P, 2])
                y0, y1, xt, x2, hb = bufs("y0", [P, D]), bufs("y1", [P, D]), bufs("xt", [P, D]), bufs("x2", [P, D]), bufs("hb", [P, D])
                junk = sbuf(st, f"junk_c{l}", [P, D])
                ss, rt = sbuf(st, f"ss_c{l}", [P, 2]), sbuf(st, f"rt_c{l}", [P, 2])
                nm = lambda s: sem(f"{s}_c{l}")
                x_in, x_out, h_out = ([nm(f"{s}{j}") for j in range(2)] for s in ("x_in", "x_out", "h_out"))
                y_in = [gather_sem(f"y_in{j}_c{l}") for j in range(2)]
                rows_in, rows_ok, ib_ok, y_used, x2_ok = nm("rows"), nm("gain"), nm("ib"), nm("y_used"), nm("x2")
                sum_ok, sqrt_ok, h_ok, tr_ok, ev_ok, dv, passed = (nm(s) for s in ("sum", "sqrt", "h", "tr", "ev", "dve", "passed"))
                norm_ok = nm("normed")

                with nc.Block() as block:
                    @block.sync
                    def _(sp):
                        if last:
                            sp.dma_start(ng[:, :], row_to_all(A["final_g"], D)).then_inc(rows_in, 16)
                            load_gate(sp, rows_in, l, 1)
                        else:
                            load_rows(sp, rows_in, l + 1, 0, A["norm_g"][l + 1, 0, :], ng[:, :])
                            load_gate(sp, rows_in, l, 1)
                        for j in range(2):
                            sp.dma_start(xt[j][:, :], x1_d[j * P:(j + 1) * P, :]).then_inc(x_in[j], 16)
                        with sp.Fori(1, nt // 2) as i:
                            for j in range(2):
                                sp.wait_ge(x2_ok, 2 * i + j - 1)
                                sp.dma_start(xt[j][:, :], x1_d[bass.ds((2 * i + j) * P, P), :]).then_inc(x_in[j], 16)

                    @block.gpsimd
                    def _(g):
                        def gather(n, j):
                            g.wait_ge(y_used, n + 1)
                            for k in range(2):
                                g.tensor_copy(ib[j][:, k:k + 1], dst[:, k, bass.ds(n, 1)]).then_inc(ib_ok, 1)
                            g.wait_ge(ib_ok, 2 * n + 2)
                            g.sem_inc(passed, 1)
                            for k, y in enumerate((y0, y1)):
                                g.indirect_dma_start(out=y[j][:, :], out_offset=None, in_=ys_d[:, :],
                                                     in_offset=bass.IndirectOffsetOnAxis(ap=ib[j][:, k:k + 1], axis=0)
                                                     ).then_inc(y_in[j], 16)

                        with g.Fori(0, nt // 2) as i:
                            for j in range(2):
                                gather(2 * i + j, j)

                    @block.vector
                    def _(v):
                        v.sem_inc(y_used, 2)
                        v.wait_ge(rows_in, 48 if last else 112)
                        if not last:
                            gain(v, ng[:, :], rows_ok)

                        def add(n, j, w, first=False):
                            link = Chain(v, dv, 6, n)
                            for k in range(2):
                                link(v.tensor_copy(wb[j][:, k:k + 1], w01[:, k, bass.ds(n, 1)]))
                            v.wait_ge(y_in[j], (n - j) * 16 + 32)
                            link(v.tensor_scalar(y0[j][:, :], y0[j][:, :], wb[j][:, 0:1], None, ALU.mult))
                            link(v.scalar_tensor_tensor(out=y1[j][:, :], in0=y1[j][:, :], scalar=wb[j][:, 1:2], in1=y0[j][:, :],
                                                        op0=ALU.mult, op1=ALU.add))
                            if not first:
                                if not last:
                                    v.wait_ge(x_out[j], (n - j) * 8)
                            v.tensor_tensor(x2[j][:, :], y1[j][:, :], gt_rows[:, w, :], ALU.mult).then_inc(y_used, 1)
                            v.wait_ge(y_used, n + 3)
                            v.wait_ge(x_in[j], (n - j) * 8 + 16)
                            v.tensor_tensor(x2[j][:, :], x2[j][:, :], xt[j][:, :], ALU.add).then_inc(x2_ok, 1)
                            v.wait_ge(x2_ok, n + 1)
                            link(v.tensor_tensor_reduce(junk[:, :], x2[j][:, :], x2[j][:, :], 1.0 / D, 0.0, ALU.mult, ALU.add,
                                                        ss[:, j:j + 1]))
                            v.sem_inc(sum_ok, 1)
                            v.wait_ge(sqrt_ok, n + 1)
                            link(v.reciprocal(ss[:, j:j + 1], rt[:, j:j + 1]))
                            link.end()
                            if not first:
                                if last:
                                    v.wait_ge(h_out[j], (n - j) * 8)
                                else:
                                    v.wait_ge(tr_ok, n - 1)
                            if last:
                                v.scalar_tensor_tensor(out=hb[j][:, :], in0=x2[j][:, :], scalar=ss[:, j:j + 1],
                                                       in1=ng[:, :], op0=ALU.mult, op1=ALU.mult).then_inc(h_ok, 1)
                            else:
                                v.scalar_tensor_tensor(out=hb[j][:, :], in0=x2[j][:, :], scalar=ss[:, j:j + 1],
                                                       in1=g_rows[:, w, :], op0=ALU.mult, op1=ALU.mult).then_inc(norm_ok, 1)
                                v.wait_ge(norm_ok, n + 1)
                                v.tensor_tensor(hb[j][:, :], hb[j][:, :], sh_rows[:, w, :], ALU.add).then_inc(h_ok, 1)

                        add(0, 0, 0, True)
                        add(1, 1, 0, True)
                        with v.Fori(1, NTL // 2) as i:
                            for j in range(2):
                                add(2 * i + j, j, 0)
                        for n in range(NTL, nt):
                            add(n, n % 2, 1)

                    @block.scalar
                    def _(a):
                        def tile(n, j, rows, first=False):
                            if not last:
                                a.wait_ge(x2_ok, n + 1)
                                a.dma_start(x2_d[rows, :], x2[j][:, :]).then_inc(x_out[j], 16)
                            a.wait_ge(sum_ok, n + 1)
                            if not first:
                                a.wait_ge(dv, 6 * (n - 2) + 6)
                            a.activation(rt[:, j:j + 1], ss[:, j:j + 1], ACT.Sqrt, bias=epst[:, :]).then_inc(sqrt_ok, 1)
                            if last:
                                a.wait_ge(h_ok, n + 1)
                                a.dma_start(out[0, rows, :], hb[j][:, :]).then_inc(h_out[j], 16)

                        def evac(n, j):
                            if not last:
                                a.wait_ge(tr_ok, n + 1)
                                a.activation(hT[:, :, bass.ds(n * P, P)], banks(2 * j, 2).rearrange("p (k c) -> p k c", k=KD),
                                             ACT.Copy).then_inc(ev_ok, 1)

                        tile(0, 0, slice(0, P), True)
                        tile(1, 1, slice(P, 2 * P), True)
                        evac(0, 0)
                        with a.Fori(1, nt // 2) as i:
                            tile(2 * i, 0, bass.ds(2 * i * P, P))
                            evac(2 * i - 1, 1)
                            tile(2 * i + 1, 1, bass.ds((2 * i + 1) * P, P))
                            evac(2 * i, 0)
                        evac(nt - 1, 1)
                        for j in range(2):
                            a.wait_ge(h_out[j] if last else x_out[j], 8 * nt)

                    if not last:
                        @block.tensor
                        def _(t):
                            t.sem_inc(ev_ok, 2)
                            with t.Fori(0, nt // 2) as i:
                                for j in range(2):
                                    n = 2 * i + j
                                    t.wait_ge(ev_ok, n + 1)
                                    transposes(t, n, j, hb, h_ok, 2 * j, ev_ok, tr_ok)

        def recurrent(hT, zT):
            CW = 4
            UPW = N + 2 * (CW - 1)
            LAT0, CTX0 = 2, L + CW - 1 + 2
            CVW = L + CW - 1 + C
            with ExitStack() as st:
                wu, wy = sbuf(st, "wu", [P, KD, LBW]), sbuf(st, "wy", [P, KD, LBW])
                wg = sbuf(st, "wg", [P, 4, 2, LBW])
                UP = [sbuf(st, f"up{o}", [P, UPW]) for o in range(2)]
                uT = [sbuf(st, f"uT{o}", [P, N]) for o in range(2)]
                cv, tr = sbuf(st, "cv", [P, CVW]), sbuf(st, "tr", [P, N])
                ti, aa, qq, hh = ([sbuf(st, f"{s}{d}", [P, N]) for d in range(2)] for s in ("ti", "aa", "qq", "hh"))
                yb, y2 = sbuf(st, "yb", [P, L]), sbuf(st, "y2", [P, L])
                bin_, cw, cb = sbuf(st, "bin", [P, 2, KD]), sbuf(st, "cw", [P, CW, KD]), sbuf(st, "cb", [P, KD])
                bg = sbuf(st, "bgate", [P, 4, KD])
                lam, z_, s_, s2, acc = (sbuf(st, x, [P, 2, KD]) for x in ("lam", "lz", "ls", "ls2", "lacc"))
                c1, nc1 = sbuf(st, "c1", [P, 2, KD]), sbuf(st, "nc1", [P, 2, KD])
                wu_in, wy_in, wg_in, p_in = sem("wu_in"), sem("wy_in"), sem("wg_in"), sem("lru_p")
                e_in, e_ok, c_ok = sem("lam_abs"), sem("lam_exp"), sem("lru_c")
                u_ps, y_ps, r_ps, i_ps = sem("u_ps"), sem("y_ps"), sem("r_ps"), sem("i_ps")
                up_ok, pad_ok, u_ok = sem("up"), sem("pads"), sem("uT")
                tr_ok, ti_ok, a_ok, t2_ok, q_ok, sq_ok = (sem(x) for x in ("lr", "li", "la", "lt2", "lq", "lsq"))
                y_ok, y2_ok, gi_ok, gt_ok, z_ok = (sem(x) for x in ("yb", "y2", "gelu_in", "gelu_t", "z"))
                dv, hd_ok, c_once = sem("lru_dve"), sem("scanned"), sem("lru_once")
                sp_passed = sem("lru_sp_passed")
                wiv = A["lru_w_in"][0].rearrange("(k p) n -> p k n", p=P)
                wgv = A["lru_w_gate"][0].rearrange("d g b (c p) n -> b p (d g) c n", p=P)
                SA, SB = banks(0, 3), banks(3, 3)

                def back(ap):
                    n = ap.ap[-1][1]
                    return bass.AP(tensor=ap.tensor, offset=ap.offset + n - 1, ap=[list(ap.ap[0]), [-1, n]])

                with nc.Block() as block:
                    @block.sync
                    def _(sp):
                        def load(b, first):
                            if not first:
                                sp.wait_ge(u_ps, 2 * b)
                                sp.sem_inc(sp_passed, 1)
                            sp.dma_start(wu[:, :, :], wiv[:, :, bass.ds(LW + b * LBW, LBW)]).then_inc(wu_in, 16)
                            if not first:
                                sp.wait_ge(y_ps, 2 * b)
                                sp.sem_inc(sp_passed, 1)
                            sp.dma_start(wy[:, :, :], wiv[:, :, bass.ds(b * LBW, LBW)]).then_inc(wy_in, 16)
                            if not first:
                                sp.wait_ge(i_ps, 4 * b + 1)
                                sp.sem_inc(sp_passed, 1)
                            for q in range(4):
                                sp.dma_start(wg[:, q, :, :], wgv[bass.ds(b, 1), :, q, :, :].rearrange("o p c n -> (o p) c n")
                                             ).then_inc(wg_in, 16)
                        sp.dma_start(lam[:, :, :], A["lru_lambda"][0].rearrange("d (k p) -> p d k", p=P)).then_inc(p_in, 16)
                        sp.dma_start(bin_[:, :, :], A["lru_b_in"][0].rearrange("(m k p) -> p m k", p=P, m=2)).then_inc(p_in, 16)
                        sp.dma_start(cw[:, :, :], A["lru_conv_w"][0].rearrange("w (k p) -> p w k", p=P)).then_inc(p_in, 16)
                        sp.dma_start(cb[:, :], A["lru_conv_b"][0].rearrange("(k p) -> p k", p=P)).then_inc(p_in, 16)
                        sp.dma_start(bg[:, :, :], A["lru_b_gate"][0].rearrange("d g (k p) -> p (d g) k", p=P)).then_inc(p_in, 16)
                        load(0, True)
                        with sp.Fori(1, LB) as b:
                            load(b, False)

                    @block.scalar
                    def _(a):
                        for s in (tr_ok, ti_ok, y2_ok):
                            a.sem_inc(s, 1)
                        a.wait_ge(e_in, 1)
                        a.activation(flat(z_[:, :, :]), flat(z_[:, :, :]), ACT.Exp, scale=-1.0).then_inc(e_ok, 1)
                        a.wait_ge(c_ok, 1)

                        def gates(b, o, d):
                            g = 4 * b + 2 * o + d
                            k = bass.ds(2 * b + o, 1)
                            a.wait_ge(r_ps, g + 1)
                            a.activation(tr[:, :], SA[:, 0:N], ACT.Tanh, bias=bg[:, 2 * d, k], scale=0.5).then_inc(tr_ok, 1)
                            a.wait_ge(i_ps, g + 2)
                            a.wait_ge(hd_ok, g + 1)
                            a.activation(ti[d][:, :], SB[:, 0:N], ACT.Tanh, bias=bg[:, 2 * d + 1, k], scale=0.5).then_inc(ti_ok, 1)
                            a.wait_ge(tr_ok, g + 2)
                            a.activation(aa[d][:, :], tr[:, :], ACT.Exp, bias=nc1[:, d, k], scale=nc1[:, d, k]).then_inc(a_ok, 1)
                            a.activation(qq[d][:, :], tr[:, :], ACT.Tanh, bias=c1[:, d, k], scale=c1[:, d, k]).then_inc(t2_ok, 1)
                            a.wait_ge(a_ok, g + 1)
                            a.wait_ge(t2_ok, g + 1)

                        def roots(b, o):
                            for d in range(2):
                                g = 4 * b + 2 * o + d
                                a.wait_ge(q_ok, g + 1)
                                a.activation(qq[d][:, :], qq[d][:, :], ACT.Sqrt, scale=2.0).then_inc(sq_ok, 1)

                        def gelu_in(b, o):
                            n = 2 * b + o
                            k = bass.ds(n, 1)
                            a.wait_ge(y_ps, n + 1)
                            a.wait_ge(z_ok, n + 1)
                            a.activation(yb[:, :], banks(6, 2), ACT.Identity, bias=bin_[:, 0, k]).then_inc(y_ok, 1)
                            a.activation(y2[:, :], banks(6, 2), ACT.Square, bias=bin_[:, 0, k]).then_inc(y2_ok, 1)
                            a.wait_ge(gi_ok, n + 1)
                            a.activation(y2[:, :], y2[:, :], ACT.Tanh, scale=(2.0 / np.pi) ** 0.5).then_inc(gt_ok, 1)

                        with a.Fori(0, LB) as b:
                            for o, src in enumerate((SA, SB)):
                                n = 2 * b + o
                                a.wait_ge(u_ps, n + 1)
                                a.wait_ge(pad_ok, n + 1)
                                bias = bin_[:, 1, bass.ds(n, 1)]
                                a.activation(UP[o][:, LAT0:LAT0 + L], src[:, 0:L], ACT.Identity, bias=bias).then_inc(up_ok, 1)
                                a.activation(UP[o][:, CTX0:CTX0 + C], src[:, L:N], ACT.Identity, bias=bias).then_inc(up_ok, 1)
                            gelu_in(b, 0)
                            gates(b, 0, 0)
                            gates(b, 0, 1)
                            roots(b, 0)
                            gelu_in(b, 1)
                            gates(b, 1, 0)
                            gates(b, 1, 1)
                            roots(b, 1)

                    @block.vector
                    def _(v):
                        n_ = [0]

                        def once(ins):
                            n_[0] += 1
                            ins.then_inc(c_once, 1)
                            v.wait_ge(c_once, n_[0])

                        v.wait_ge(p_in, 80)
                        L2 = lambda x: flat(x[:, :, :])
                        once(v.tensor_scalar(L2(s_), L2(lam), -1.0, 0.0, ALU.mult, ALU.max))
                        once(v.tensor_scalar(L2(s2), L2(lam), 0.0, None, ALU.max))
                        v.tensor_tensor(L2(z_), L2(s_), L2(s2), ALU.add).then_inc(e_in, 1)
                        v.wait_ge(e_ok, 1)
                        once(v.tensor_scalar(L2(s2), L2(z_), 2.0, None, ALU.add))
                        once(v.reciprocal(L2(s2), L2(s2)))
                        once(v.tensor_tensor(L2(z_), L2(z_), L2(s2), ALU.mult))
                        once(v.tensor_tensor(L2(s2), L2(z_), L2(z_), ALU.mult))
                        once(v.memset(L2(acc), 1.0 / 17))
                        for m in range(15, 0, -2):
                            once(v.tensor_tensor(L2(acc), L2(acc), L2(s2), ALU.mult))
                            once(v.tensor_scalar(L2(acc), L2(acc), 1.0 / m, None, ALU.add))
                        once(v.tensor_tensor(L2(acc), L2(acc), L2(z_), ALU.mult))
                        once(v.scalar_tensor_tensor(out=L2(acc), in0=L2(acc), scalar=2.0, in1=L2(s_), op0=ALU.mult, op1=ALU.add))
                        once(v.tensor_scalar(L2(c1), L2(acc), 4.0, None, ALU.mult))
                        once(v.tensor_scalar(L2(nc1), L2(acc), -4.0, None, ALU.mult))
                        once(v.tensor_scalar(flat(bg[:, :, :]), flat(bg[:, :, :]), 0.5, None, ALU.mult))
                        for o in range(2):
                            once(v.memset(UP[o][:, :], 0.0))
                            v.sem_inc(pad_ok, 1)
                        v.sem_inc(c_ok, 1)
                        v.sem_inc(z_ok, 1)
                        v.sem_inc(hd_ok, 1)
                        v.sem_inc(hd_ok, 1)

                        def conv(b, o, link):
                            n = 2 * b + o
                            k = bass.ds(n, 1)
                            v.wait_ge(up_ok, 2 * n + 2)
                            link(v.tensor_scalar(cv[:, :], UP[o][:, 0:CVW], cw[:, 0, k], cb[:, k], ALU.mult, ALU.add))
                            for w in range(1, CW - 1):
                                link(v.scalar_tensor_tensor(out=cv[:, :], in0=UP[o][:, w:w + CVW], scalar=cw[:, w, k],
                                                            in1=cv[:, :], op0=ALU.mult, op1=ALU.add))
                            w = CW - 1
                            v.wait_ge(i_ps, 4 * b + 1)
                            link(v.scalar_tensor_tensor(out=uT[o][:, 0:L], in0=UP[o][:, w:w + L], scalar=cw[:, w, k],
                                                        in1=cv[:, 0:L], op0=ALU.mult, op1=ALU.add))
                            c0 = L + CW - 1
                            link(v.scalar_tensor_tensor(out=uT[o][:, L:N], in0=UP[o][:, w + c0:w + c0 + C], scalar=cw[:, w, k],
                                                        in1=cv[:, c0:c0 + C], op0=ALU.mult, op1=ALU.add))
                            v.sem_inc(pad_ok, 1)
                            v.sem_inc(u_ok, 1)

                        def gelu_mid(b, o, link):
                            n = 2 * b + o
                            v.wait_ge(y2_ok, n + 2)
                            link(v.tensor_scalar(y2[:, :], y2[:, :], 0.044715, 1.0, ALU.mult, ALU.add))
                            v.wait_ge(y_ok, n + 1)
                            v.tensor_tensor(y2[:, :], y2[:, :], yb[:, :], ALU.mult).then_inc(gi_ok, 1)

                        def decay(b, o, d, link):
                            g = 4 * b + 2 * o + d
                            v.wait_ge(t2_ok, g + 1)
                            link(v.tensor_scalar(hh[d][:, :], qq[d][:, :], 1.0, None, ALU.add))
                            link(v.reciprocal(hh[d][:, :], hh[d][:, :]))
                            v.tensor_tensor(qq[d][:, :], qq[d][:, :], hh[d][:, :], ALU.mult).then_inc(q_ok, 1)
                            v.wait_ge(ti_ok, g + 2)
                            link(v.scalar_tensor_tensor(out=ti[d][:, :], in0=ti[d][:, :], scalar=1.0, in1=uT[o][:, :],
                                                        op0=ALU.add, op1=ALU.mult))

                        def scan(b, o, d, link):
                            g = 4 * b + 2 * o + d
                            v.wait_ge(sq_ok, g + 1)
                            v.wait_ge(a_ok, g + 1)
                            link(v.scalar_tensor_tensor(out=qq[d][:, :], in0=ti[d][:, :], scalar=0.5, in1=qq[d][:, :],
                                                        op0=ALU.mult, op1=ALU.mult))
                            turn = back if d else (lambda ap: ap)
                            link(v.tensor_tensor_scan(turn(hh[d][:, L:N]), turn(aa[d][:, L:N]), turn(qq[d][:, L:N]), 0.0,
                                                      ALU.mult, ALU.add))
                            end = L if d else N - 1
                            link(v.tensor_tensor_scan(turn(hh[d][:, 0:L]), turn(aa[d][:, 0:L]), turn(qq[d][:, 0:L]),
                                                      hh[d][:, end:end + 1], ALU.mult, ALU.add))
                            v.sem_inc(hd_ok, 1)

                        def close(b, o, link):
                            n = 2 * b + o
                            link(v.tensor_tensor(hh[0][:, 0:L], hh[0][:, 0:L], hh[1][:, 0:L], ALU.add))
                            v.wait_ge(gt_ok, n + 1)
                            link(v.scalar_tensor_tensor(out=y2[:, :], in0=y2[:, :], scalar=1.0, in1=yb[:, :],
                                                        op0=ALU.add, op1=ALU.mult))
                            v.scalar_tensor_tensor(out=zT[:, bass.ds(n, 1), :].rearrange("p o n -> p (o n)"), in0=y2[:, :],
                                                   scalar=0.5, in1=hh[0][:, 0:L], op0=ALU.mult, op1=ALU.mult).then_inc(z_ok, 1)

                        with v.Fori(0, LB) as b:
                            link = Chain(v, dv, 2 * (5 + 1 + 2 * 3 + 2 * 3 + 2), b)
                            conv(b, 0, link)
                            conv(b, 1, link)
                            for o in range(2):
                                gelu_mid(b, o, link)
                                decay(b, o, 0, link)
                                decay(b, o, 1, link)
                                scan(b, o, 0, link)
                                scan(b, o, 1, link)
                                close(b, o, link)
                            link.end()

                    @block.tensor
                    def _(t):
                        def product(n, w, o, dst, cols, s):
                            for c in range(0, cols, 512):
                                wd = min(512, cols - c)
                                for k in range(KD):
                                    mm = t.matmul(dst[:, c:c + wd], w[:, k, o * P:(o + 1) * P], hT[:, k, c:c + wd],
                                                  start=(k == 0), stop=(k == KD - 1))
                            mm.then_inc(s, 1)

                        def gates(b, o, d):
                            g = 4 * b + 2 * o + d
                            for q, dst, free, s in ((2 * d, SA, tr_ok, r_ps), (2 * d + 1, SB, ti_ok, i_ps)):
                                t.wait_ge(free, g + 1)
                                for c in range(0, N, 512):
                                    wd = min(512, N - c)
                                    for k in range(2):
                                        mm = t.matmul(dst[:, c:c + wd], wg[:, q, k, o * P:(o + 1) * P], uT[k][:, c:c + wd],
                                                      start=(k == 0), stop=(k == 1))
                                mm.then_inc(s, 1)

                        t.sem_inc(i_ps, 1)
                        with t.Fori(0, LB) as b:
                            t.wait_ge(wu_in, 16 * b + 16)
                            t.wait_ge(tr_ok, 4 * b + 1)
                            product(2 * b, wu, 0, SA, N, u_ps)
                            t.wait_ge(ti_ok, 4 * b + 1)
                            product(2 * b + 1, wu, 1, SB, N, u_ps)
                            t.wait_ge(wy_in, 16 * b + 16)
                            t.wait_ge(y2_ok, 2 * b + 1)
                            product(2 * b, wy, 0, banks(6, 2), L, y_ps)
                            t.wait_ge(wg_in, 64 * b + 64)
                            t.wait_ge(u_ok, 2 * b + 2)
                            t.wait_ge(up_ok, 4 * b + 4)
                            gates(b, 0, 0)
                            gates(b, 0, 1)
                            t.wait_ge(y2_ok, 2 * b + 2)
                            product(2 * b + 1, wy, 1, banks(6, 2), L, y_ps)
                            gates(b, 1, 0)
                            gates(b, 1, 1)

        def routing_tables(stack, l, nt):
            return (sbuf(stack, f"dst{l}", [P, 2, nt], I32), sbuf(stack, f"w01_{l}", [P, 2, nt]),
                    sbuf(stack, f"item{l}", [P, ITEMS], I32), sbuf(stack, f"item_slots{l}", [P, ITEMS], I32),
                    sbuf(stack, f"n_pairs{l}", [P, 1], I32))

        with ExitStack() as layer:
            RL = sbuf(layer, "RL0", [P, NT, NR])
            tabs = routing_tables(layer, 0, NT)
            with ExitStack() as att:
                OT = sbuf(att, "OT", [P, KD, N])
                with ExitStack() as sth:
                    hT = sbuf(sth, "hT", [P, KD, N])
                    first_norm(hT)
                    if stop == 1:
                        return
                    attention(hT, OT)
                    if stop == 2:
                        return
                projection(0, NT, OT, A["na_w_o"][0], A["na_b_o"][0], RL)
                if stop == 3:
                    return
            routing(0, NT, RL, tabs)
            if stop == 4:
                return
            experts(0, tabs)
            if stop == 5:
                return
            RL1 = sbuf(layer, "RL1", [P, NTL, NR])
            tabs1 = routing_tables(layer, 1, NTL)
            with ExitStack() as lru:
                zT = sbuf(lru, "zT", [P, KD, L])
                with ExitStack() as sth:
                    hT = sbuf(sth, "hT1", [P, KD, N])
                    combine(0, NT, tabs, hT)
                    semaphores_anew()
                    if stop == 6:
                        return
                    recurrent(hT, zT)
                    if stop == 7:
                        return
                projection(1, NTL, zT, A["lru_w_o"][0], A["lru_b_o"][0], RL1)
                if stop == 8:
                    return
            routing(1, NTL, RL1, tabs1)
            experts(1, tabs1)
            combine(1, NTL, tabs1, None)


_INS = ["x", "c", "ctx", "c_ctx", "ada_w", "ada_b", "norm_g", "na_w_qkv", "na_b_qkv", "na_rpb", "na_w_o", "na_b_o",
        "lru_w_in", "lru_b_in", "lru_conv_w", "lru_conv_b", "lru_w_gate", "lru_b_gate", "lru_lambda", "lru_w_o",
        "lru_b_o", "moe_w_group", "moe_b_group", "moe_w_expert", "moe_b_expert", "moe_w1", "moe_w3", "moe_w2", "final_g"]


def kernel(**inputs):
    import concourse.bacc as bacc
    from concourse.bass_utils import run_bass_kernel_spmd

    nc = bacc.Bacc("TRN2", target_bir_lowering=False, num_devices=1)
    arrays, aps = {}, {}
    for name in _INS:
        a = np.ascontiguousarray(inputs[name])
        if name == "na_rpb":
            side = (RPB_W - a.shape[-1]) // 2
            a = np.pad(a, ((0, 0), (0, 0), (0, 0), (side, side)))
        arrays[f"in_{name}"] = a
        aps[name] = nc.dram_tensor(f"in_{name}", a.shape, F32, kind="ExternalInput").ap()
    out = nc.dram_tensor("out", (1, L, D), F32, kind="ExternalOutput").ap()
    program(nc, aps, out)
    r = run_bass_kernel_spmd(nc, [arrays], core_ids=[0])
    return r.results[0]["out"]
```

```python
from contextlib import ExitStack

import numpy as np

import concourse.bass as bass
from concourse import mybir

F32 = mybir.dt.float32
F32R = mybir.dt.float32r
I32 = mybir.dt.int32
ALU = mybir.AluOpType
ACT = mybir.ActivationFunctionType
AX = mybir.AxisListType.X

P = 128
D = 1024
KD = D // P
L = 1024
C = 256
N = L + C
NTL, NTC = L // P, C // P
NT = NTL + NTC
GRID_W = 64
ROWS = L // GRID_W
HEADS, HD = 16, 64
PAIRS = HEADS // 2
WIN_H, WIN_W = 8, 16
RPB_W = 2 * GRID_W - 1
GROUPS, EPG = 4, 8
EXPERTS = GROUPS * EPG
FF = 512
KF = FF // P
NR = GROUPS + EXPERTS
MAX_ITEMS = EXPERTS + (2 * N - 1) // P
ITEMS = 56
SLOTS = ITEMS * P
NMOD = 6
EPS = 1e-6
NEG = -1e30
LW = 1024
LB = 4
LBW = LW // LB


class Chain:

    def __init__(self, eng, sem, per, n):
        self.eng, self.sem, self.per, self.n, self.k = eng, sem, per, n, 0

    def __call__(self, ins):
        self.k += 1
        ins.then_inc(self.sem, 1)
        self.eng.wait_ge(self.sem, self.n * self.per + self.k)

    def end(self):
        assert self.k == self.per, (self.k, self.per)


def flat(ap):
    return ap.rearrange("p a b -> p (a b)")


def row_to_all(ap_1d, n):
    return bass.AP(tensor=ap_1d.tensor, offset=ap_1d.offset, ap=[[0, P], [1, n]])


def expand(ap, *spots):
    dims = [list(d) for d in ap.ap]
    for place, size in spots:
        dims.insert(place, [0, size])
    return bass.AP(tensor=ap.tensor, offset=ap.offset, ap=dims)


def rows_reversed(ap, rows):
    return bass.AP(tensor=ap.tensor, offset=ap.offset + GRID_W - 1, ap=[list(ap.ap[0]), [GRID_W, rows], [-1, GRID_W]])


def three(t, out_, lh, ll, wh, wl, start, stop):
    t.matmul(out_, lh, wh, start=start, stop=False)
    t.matmul(out_, lh, wl, start=False, stop=False)
    return t.matmul(out_, ll, wh, start=False, stop=stop)


def program(nc, A, out, stop=99):
    root = ExitStack()
    with root:
        def sbuf(stack, name, shape, dt=F32):
            return stack.enter_context(nc.sbuf_tensor(name, shape, dt))

        sems, taken = ExitStack(), []
        root.enter_context(sems)

        def sem(name):
            taken.append(sems.enter_context(nc.semaphore(name)))
            return taken[-1]

        def gather_sem(name):
            return root.enter_context(nc.semaphore(name))

        def semaphores_anew():
            for s in taken:
                nc.gpsimd.sem_clear(s)
            nc.all_engine_barrier()
            taken.clear()
            sems.close()

        root.enter_context(nc.allow_non_contiguous_dma("columns of small vectors and of the router"))
        dram = lambda name, shape, dt=F32: nc.dram_tensor(name, shape, dt, kind="Internal").ap()

        mod_d = dram("mod_d", (2, 2 * NMOD * D))
        x1_d = dram("x1_d", (N, D))
        x2_d = dram("x2_d", (N, D))
        h2_d = dram("h2_d", (N, D))
        slot_d = [dram(f"slot_d{l}", (P * ITEMS, 1), I32) for l in range(2)]
        ys_d = dram("ys_d", (SLOTS, D))

        PS = root.enter_context(nc.psum_tensor("PS", [P, 8, 512], F32))
        banks = lambda a, n: flat(PS[:, a:a + n, :])

        ident = sbuf(root, "ident", [P, P])
        ones = sbuf(root, "ones", [P, P])
        ltri = sbuf(root, "ltri", [P, P])
        epst = sbuf(root, "epst", [P, 1])
        g_rows = sbuf(root, "g_rows", [P, 2, D])
        sh_rows = sbuf(root, "sh_rows", [P, 2, D])
        gt_rows = sbuf(root, "gt_rows", [P, 2, D])

        CH = 2 * NMOD * D // 512
        AWR = 4
        with ExitStack() as st:
            cond = sbuf(st, "cond", [P, 2, KD])
            th = sbuf(st, "th", [P, 2, KD])
            csil = sbuf(st, "csil", [P, 2, KD])
            chi, clo = sbuf(st, "chi", [P, 2, KD], F32R), sbuf(st, "clo", [P, 2, KD], F32R)
            aw = [sbuf(st, f"aw{r}", [P, KD, 512]) for r in range(AWR)]
            awhi = [sbuf(st, f"awhi{j}", [P, KD, 512], F32R) for j in range(2)]
            awlo = [sbuf(st, f"awlo{j}", [P, KD, 512], F32R) for j in range(2)]
            ab = sbuf(st, "ab", [2, 2 * NMOD * D])
            mo = [sbuf(st, f"mo{j}", [2, 512]) for j in range(2)]
            c_in, c_th, c_si, a_ch, ab_in = sem("c_in"), sem("c_th"), sem("c_si"), sem("a_ch"), sem("ab_in")
            ch_ok, cl_ok, hi_ok, lo_ok = sem("c_high"), sem("c_low"), sem("ada_high"), sem("ada_low")
            w_in = [sem(f"ada_in{r}") for r in range(AWR)]
            w_used = sem("ada_used")
            m_ready, m_out = sem("mod_ready"), [sem(f"mod_out{j}") for j in range(2)]
            k_id, k_done = sem("k_id"), sem("k_done")
            with nc.Block() as block:
                @block.sync
                def _(sp):
                    sp.dma_start(cond[:, 0, :], A["c"].rearrange("o (k p) -> p (o k)", p=P)).then_inc(c_in, 16)
                    sp.dma_start(cond[:, 1, :], A["c_ctx"].rearrange("(k p) -> p k", p=P)).then_inc(c_in, 16)
                    for r in range(2):
                        sp.dma_start(ab[r:r + 1, :], A["ada_b"].rearrange("(o l) n -> o (l n)", o=1)).then_inc(ab_in, 16)
                    for l in range(2):
                        wv = A["ada_w"][l].rearrange("(k p) n -> p k n", p=P)
                        with sp.Fori(0, CH // 2 // AWR) as i:
                            for q in range(AWR):
                                sp.wait_ge(lo_ok, l * CH // 2 + AWR * i + q + 1)
                                sp.dma_start(aw[q][:, :, :], wv[:, :, bass.ds((AWR * i + q) * 512, 512)]).then_inc(w_in[q], 16)

                @block.gpsimd
                def _(g):
                    g.memset(ones[:, :], 1.0).then_inc(k_id, 1)
                    g.memset(epst[:, :], EPS).then_inc(k_id, 1)
                    g.memset(ident[:, :], 0.0).then_inc(k_id, 1)
                    g.wait_ge(k_id, 3)
                    g.affine_select(out=ident[:, :], in_=ident[:, :], compare_op=ALU.not_equal, fill=1.0,
                                    base=0, pattern=[[-1, P]], channel_multiplier=1).then_inc(k_done, 1)
                    g.affine_select(out=ltri[:, :], in_=ones[:, :], compare_op=ALU.is_gt, fill=0.0,
                                    base=0, pattern=[[1, P]], channel_multiplier=-1).then_inc(k_done, 1)

                @block.scalar
                def _(a):
                    a.wait_ge(c_in, 32)
                    a.activation(flat(th[:, :, :]), flat(cond[:, :, :]), ACT.Tanh, scale=0.5).then_inc(c_th, 1)
                    a.wait_ge(c_si, 1)
                    a.activation(flat(chi[:, :, :]), flat(csil[:, :, :]), ACT.Copy).then_inc(ch_ok, 1)

                    def high(n, q):
                        j = q % 2
                        a.wait_ge(w_in[q], (n - q) * 4 + 16)
                        a.wait_ge(w_used, n + 1)
                        a.activation(flat(awhi[j][:, :, :]), flat(aw[q][:, :, :]), ACT.Copy).then_inc(hi_ok, 1)

                    def store(n, j):
                        a.wait_ge(m_ready, n + 3)
                        a.dma_start(mod_d[:, bass.ds(n * 512, 512)], mo[j][:, :]).then_inc(m_out[j], 16)

                    high(0, 0)
                    high(1, 1)
                    for n in (2, 3):
                        high(n, n)
                        store(n - 2, n - 2)
                    with a.Fori(1, CH // AWR) as i:
                        for q in range(AWR):
                            high(AWR * i + q, q)
                            store(AWR * i + q - 2, q % 2)
                    for j in range(2):
                        store(CH - 2 + j, j)
                    for j in range(2):
                        a.wait_ge(m_out[j], 8 * CH)

                @block.vector
                def _(v):
                    v.sem_inc(lo_ok, AWR)
                    v.sem_inc(m_ready, 2)
                    v.wait_ge(c_th, 1)
                    v.scalar_tensor_tensor(out=flat(csil[:, :, :]), in0=flat(th[:, :, :]), scalar=1.0,
                                           in1=flat(cond[:, :, :]), op0=ALU.add, op1=ALU.mult).then_inc(a_ch, 1)
                    v.wait_ge(a_ch, 1)
                    v.tensor_scalar(flat(csil[:, :, :]), flat(csil[:, :, :]), 0.5, None, ALU.mult).then_inc(c_si, 1)
                    v.wait_ge(ch_ok, 1)
                    v.tensor_tensor(flat(clo[:, :, :]), flat(csil[:, :, :]), flat(chi[:, :, :]).bitcast(F32),
                                    ALU.subtract).then_inc(cl_ok, 1)

                    def low(n, q):
                        j = q % 2
                        v.wait_ge(hi_ok, n + 1)
                        v.tensor_tensor(flat(awlo[j][:, :, :]), flat(aw[q][:, :, :]), flat(awhi[j][:, :, :]).bitcast(F32),
                                        ALU.subtract).then_inc(lo_ok, 1)

                    def bias(n, j, first=False):
                        v.wait_ge(w_used, n + 3)
                        if not first:
                            v.wait_ge(m_out[j], (n - j) * 8)
                        v.tensor_tensor(mo[j][:, :], PS[0:2, j, :], ab[:, bass.ds(n * 512, 512)], ALU.add).then_inc(m_ready, 1)

                    low(0, 0)
                    v.wait_ge(ab_in, 32)
                    low(1, 1)
                    bias(0, 0, True)
                    low(2, 2)
                    bias(1, 1, True)
                    low(3, 3)
                    bias(2, 0)
                    with v.Fori(1, CH // AWR) as i:
                        for q in range(AWR):
                            low(AWR * i + q, q)
                            bias(AWR * i + q - 1, (q - 1) % 2)
                    bias(CH - 1, 1)

                @block.tensor
                def _(t):
                    t.sem_inc(w_used, 2)
                    t.wait_ge(cl_ok, 1)
                    with t.Fori(0, CH // 2) as i:
                        for j in range(2):
                            n = 2 * i + j
                            t.wait_ge(lo_ok, n + AWR + 1)
                            t.wait_ge(m_ready, n + 1)
                            for k in range(KD):
                                mm = three(t, PS[0:2, j, :], chi[:, :, k], clo[:, :, k], awhi[j][:, k, :], awlo[j][:, k, :],
                                           k == 0, k == KD - 1)
                            mm.then_inc(w_used, 1)

        if stop == 0:
            return

        def load_rows(eng, s, l, sub, ng_row, tmp_ng):
            for w in range(2):
                eng.dma_start(sh_rows[:, w, :], row_to_all(mod_d[w, (NMOD * l + 3 * sub) * D:], D)).then_inc(s, 16)
                eng.dma_start(g_rows[:, w, :], row_to_all(mod_d[w, (NMOD * l + 3 * sub + 1) * D:], D)).then_inc(s, 16)
            eng.dma_start(tmp_ng, row_to_all(ng_row, D)).then_inc(s, 16)

        def load_gate(eng, s, l, sub):
            for w in range(2):
                eng.dma_start(gt_rows[:, w, :], row_to_all(mod_d[w, (NMOD * l + 3 * sub + 2) * D:], D)).then_inc(s, 16)

        def gain(v, tmp_ng, s):
            for w in range(2):
                v.scalar_tensor_tensor(out=g_rows[:, w, :], in0=g_rows[:, w, :], scalar=1.0, in1=tmp_ng,
                                       op0=ALU.add, op1=ALU.mult).then_inc(s, 1)
            v.wait_ge(s, 2)


        def transposes(t, n, j, hb, hs_ready, ps0, evac_done, tr_done):
            t.wait_ge(hs_ready, n + 1)
            for k in range(KD):
                mm = t.transpose(banks(ps0, 2)[:, k * P:(k + 1) * P], hb[j][:, k * P:(k + 1) * P], ident[:, :])
            mm.then_inc(tr_done, 1)

        def first_norm(hT):
            with ExitStack() as st:
                ng = sbuf(st, "ng_b", [P, D])
                XR = 4
                xt = [sbuf(st, f"xt_b{r}", [P, D]) for r in range(XR)]
                hb = [sbuf(st, f"hb_b{j}", [P, D]) for j in range(2)]
                junk = sbuf(st, "junk_b", [P, D])
                ss, rt = sbuf(st, "ss_b", [P, 2]), sbuf(st, "rt_b", [P, 2])
                rows_in, rows_ok = sem("b_rows"), sem("b_gain")
                x_in = [sem(f"b_x{r}") for r in range(XR)]
                sum_ok, sqrt_ok, h_ok, tr_ok, ev_ok = sem("b_sum"), sem("b_sqrt"), sem("b_h"), sem("b_tr"), sem("b_ev")
                dv = sem("b_dve")
                with nc.Block() as block:
                    @block.sync
                    def _(sp):
                        for n in range(NT):
                            if n == 2:
                                load_rows(sp, rows_in, 0, 0, A["norm_g"][0, 0, :], ng[:, :])
                            src = A["x"][0, n * P:(n + 1) * P, :] if n < NTL else A["ctx"][0, (n - NTL) * P:(n - NTL + 1) * P, :]
                            if n >= XR:
                                sp.wait_ge(h_ok, n - XR + 1)
                            sp.dma_start(xt[n % XR][:, :], src).then_inc(x_in[n % XR], 16)

                    @block.vector
                    def _(v):
                        def squares(n):
                            x, j = xt[n % XR], n % 2
                            v.wait_ge(x_in[n % XR], n // XR * 16 + 16)
                            v.tensor_tensor_reduce(junk[:, :], x[:, :], x[:, :], 1.0 / D, 0.0, ALU.mult, ALU.add,
                                                   ss[:, j:j + 1]).then_inc(sum_ok, 1)
                            v.wait_ge(sum_ok, n + 1)

                        def norm(n, w):
                            j = n % 2
                            link = Chain(v, dv, 2, n)
                            v.wait_ge(sqrt_ok, n + 1)
                            link(v.reciprocal(ss[:, j:j + 1], rt[:, j:j + 1]))
                            if n >= 2:
                                v.wait_ge(tr_ok, n - 1)
                            link(v.scalar_tensor_tensor(out=hb[j][:, :], in0=xt[n % XR][:, :], scalar=ss[:, j:j + 1],
                                                        in1=g_rows[:, w, :], op0=ALU.mult, op1=ALU.mult))
                            v.tensor_tensor(hb[j][:, :], hb[j][:, :], sh_rows[:, w, :], ALU.add).then_inc(h_ok, 1)

                        squares(0)
                        v.wait_ge(rows_in, 80)
                        gain(v, ng[:, :], rows_ok)
                        for n in range(NT):
                            if n + 1 < NT:
                                squares(n + 1)
                            norm(n, 0 if n < NTL else 1)

                    @block.scalar
                    def _(a):
                        def root_(n, j, first=False):
                            a.wait_ge(sum_ok, n + 1)
                            if not first:
                                a.wait_ge(dv, 2 * (n - 2) + 1)
                            a.activation(rt[:, j:j + 1], ss[:, j:j + 1], ACT.Sqrt, bias=epst[:, :]).then_inc(sqrt_ok, 1)

                        def evac(n, j):
                            a.wait_ge(tr_ok, n + 1)
                            a.activation(hT[:, :, bass.ds(n * P, P)], banks(2 * j, 2).rearrange("p (k c) -> p k c", k=KD),
                                         ACT.Copy).then_inc(ev_ok, 1)

                        root_(0, 0, True)
                        root_(1, 1, True)
                        evac(0, 0)
                        root_(2, 0)
                        evac(1, 1)
                        with a.Fori(1, NTL // 2) as i:
                            root_(2 * i + 1, 1)
                            evac(2 * i, 0)
                            root_(2 * i + 2, 0)
                            evac(2 * i + 1, 1)
                        root_(NTL + 1, 1)
                        evac(NTL, 0)
                        evac(NTL + 1, 1)

                    @block.tensor
                    def _(t):
                        t.sem_inc(ev_ok, 2)
                        with t.Fori(0, NT // 2) as i:
                            for j in range(2):
                                n = 2 * i + j
                                t.wait_ge(ev_ok, n + 1)
                                transposes(t, n, j, hb, h_ok, 2 * j, ev_ok, tr_ok)

        UNITS = 2 * NT
        NB = 2 * WIN_H - 2
        QKV = 9
        STEPS = QKV + 3
        SLOTS_OF_W = {1: 0, 3: 1, 5: 2, 7: 3, 9: 4, 11: 5, 13: 6, 15: 7, 16: 8, 17: QKV, 19: QKV + 1}
        PIECES = ((0, 512), (512, 512), (1024, 256))
        NI = 10

        def window(t):
            if 2 <= t <= 5:
                return 2 * t - 4, NI, NB
            base = 0 if t < 2 else ROWS - WIN_H
            return base, WIN_H, base - 2 * t + 7 - 1

        def attention(hT, OT):
            with ExitStack() as st:
                slab = [sbuf(st, f"slab{m}", [P, KD, P]) for m in range(3)]
                qT, kT = ([sbuf(st, f"{x}{b}", [P, N]) for b in range(2)] for x in ("qT", "kT"))
                V = [sbuf(st, f"V{b}", [P, NT, P]) for b in range(2)]
                raw = [sbuf(st, f"rpb_raw{j}", [P, NB, GRID_W]) for j in range(2)]
                tab = [sbuf(st, f"rpb_tab{j}", [P, NB + NI, GRID_W]) for j in range(2)]
                cmask = sbuf(st, "cmask", [P, GRID_W])
                prob = [sbuf(st, f"prob{b}", [P, 7 * P]) for b in range(2)]
                probT = [sbuf(st, f"probT{b}", [P, 7 * P]) for b in range(2)]
                osb = sbuf(st, "osb", [P, NT, P])
                sums = sbuf(st, "sums", [P, UNITS])
                small = sbuf(st, "small", [P, 2, 4])
                bq = sbuf(st, "bq", [P, 3, PAIRS])
                sl_in = [sem(f"sl_in{m}") for m in range(3)]
                w_ps, w_used = sem("w_ps"), sem("w_used")
                rb_in = [sem(f"rb_in{j}") for j in range(2)]
                bt_ok, mk, b_in, b_ok = sem("bt_ok"), sem("mask"), sem("bq_in"), sem("bq_ok")
                s_ok, neg_ok, exp_ok, pt_ok = sem("scores"), sem("negmax"), sem("exp"), sem("pT_ps")
                pa_ok, pd_ok = sem("pT_act"), sem("pT_dve")
                o_ok, on_ok = sem("o_ps"), sem("o_norm")
                dv, pc = sem("at_dve"), sem("at_pool")
                zero, zr_ok, cl_ok = sbuf(st, "zero", [P, D]), sem("zero"), sem("ys_cleared")
                v_passed, g_passed, a_passed = (sem(f"at_{x}_passed") for x in ("dve", "pool", "act"))
                toep = bass.AP(tensor=A["na_rpb"].tensor, offset=A["na_rpb"].offset,
                               ap=[[15 * RPB_W, HEADS], [1, GRID_W], [RPB_W, 15], [1, GRID_W]])
                wq = A["na_w_qkv"][0].rearrange("(k p) n -> p k n", p=P)
                S = [banks(0, 2), banks(2, 2)]
                PT = banks(4, 2)
                O, W = PS[:, 6, :], PS[:, 7, :]

                def uses(h, last):
                    for u in range(UNITS):
                        if u in SLOTS_OF_W:
                            s = SLOTS_OF_W[u]
                            if not last:
                                yield u, s, QKV + STEPS * h + s
                            elif s >= QKV:
                                yield u, s, QKV + STEPS * h + s - QKV
                    yield UNITS, STEPS - 1, QKV + STEPS * h + (2 if last else STEPS - 1)

                def turns(eng, pair):
                    with eng.Fori(0, PAIRS // 2 - 1) as i:
                        for hp in range(2):
                            pair(2 * i + hp, hp, False)
                    pair(PAIRS - 2, 0, False)
                    pair(PAIRS - 1, 1, True)

                def keys(t):
                    nw = window(t)[1] * GRID_W if t < NTL else 0
                    return nw, nw + C

                with nc.Block() as block:
                    @block.sync
                    def _(sp):
                        sp.dma_start(bq[:, :, :], A["na_b_qkv"][0].rearrange("(m h p) -> p m h", p=P, m=3)).then_inc(b_in, 16)

                        def load_pair(h, first=False, second=False):
                            for m in range(3):
                                if not first:
                                    sp.wait_ge(w_ps, 3 * m + 3 if second else STEPS * h - STEPS + 3 * m)
                                sp.dma_start(slab[m][:, :, :], wq[:, :, bass.ds(m * D + h * P, P)]).then_inc(sl_in[m], 16)
                            for j in range(2):
                                if not first:
                                    sp.wait_ge(bt_ok, 2 * (h - 1) + j + 1)
                                for a in range(2):
                                    src = toep[bass.ds(2 * h + j, 1), :, 1 - a:1 - a + NB, :]
                                    sp.dma_start(raw[j][a * GRID_W:(a + 1) * GRID_W, :, :],
                                                 src.rearrange("o c m k -> (o c) m k")).then_inc(rb_in[j], 16)

                        def clear_slots(h):
                            n = ITEMS // PAIRS
                            dst = ys_d[bass.ds(h * n * P, n * P), :].rearrange("(i p) d -> p i d", p=P)
                            sp.dma_start(dst, expand(zero[:, :], (1, n))).then_inc(cl_ok, 16)

                        load_pair(0, first=True)
                        sp.wait_ge(zr_ok, 1)
                        clear_slots(0)
                        load_pair(1, second=True)
                        clear_slots(1)
                        with sp.Fori(2, PAIRS) as h:
                            load_pair(h)
                            clear_slots(h)
                        sp.wait_ge(cl_ok, 16 * PAIRS)

                    @block.gpsimd
                    def _(g):
                        g.memset(zero[:, :], 0.0).then_inc(zr_ok, 1)
                        g.memset(cmask[:, :], 0.0).then_inc(mk, 1)
                        g.wait_ge(mk, 1)
                        lo = WIN_W // 2
                        for a in range(2):
                            part = cmask[a * GRID_W:(a + 1) * GRID_W, :]
                            g.affine_select(out=part[:, 0:GRID_W - WIN_W], in_=part[:, 0:GRID_W - WIN_W], compare_op=ALU.is_ge,
                                            fill=NEG, base=lo - (GRID_W - 1), pattern=[[1, GRID_W - WIN_W]],
                                            channel_multiplier=1).then_inc(mk, 1)
                            g.wait_ge(mk, 2 * a + 2)
                            g.affine_select(out=part[:, WIN_W:], in_=part[:, WIN_W:], compare_op=ALU.is_ge,
                                            fill=NEG, base=GRID_W - 1 + lo - 1 - WIN_W, pattern=[[-1, GRID_W - WIN_W]],
                                            channel_multiplier=-1).then_inc(mk, 1)
                            g.wait_ge(mk, 2 * a + 3)
                        cm = cmask[:, :]
                        cmb = bass.AP(tensor=cm.tensor, offset=cm.offset, ap=[list(cm.ap[0]), [0, NB], [1, GRID_W]])

                        def table(h, j, first):
                            g.wait_ge(rb_in[j], 32 * h + 32)
                            if not first:
                                g.wait_ge(neg_ok, UNITS * (h - 1) + NT * j + NTL)
                            link = Chain(g, pc, 2, 2 * h + j)
                            link(g.tensor_tensor(tab[j][:, 0:NB, :], raw[j][:, :, :], cmb, ALU.add))
                            g.sem_inc(g_passed, 1)
                            link(g.tensor_copy(tab[j][:, NB:NB + NI, :], tab[j][:, 2:2 + NI, :]))
                            g.sem_inc(g_passed, 1)
                            g.memset(tab[j][0:GRID_W, NB + 8:NB + 10, :], NEG).then_inc(mk, 1)
                            g.memset(tab[j][GRID_W:P, NB:NB + 1, :], NEG).then_inc(mk, 1)
                            g.memset(tab[j][GRID_W:P, NB + 9:NB + 10, :], NEG).then_inc(mk, 1)
                            g.wait_ge(mk, 5 + 3 * (2 * h + j) + 3)
                            g.sem_inc(bt_ok, 1)

                        for j in range(2):
                            table(0, j, True)
                        with g.Fori(1, PAIRS) as h:
                            for j in range(2):
                                table(h, j, False)

                    @block.scalar
                    def _(a):
                        a.wait_ge(b_in, 16)
                        a.activation(bq[:, 0, :], bq[:, 0, :], ACT.Copy, scale=HD ** -0.5).then_inc(b_ok, 1)
                        a.wait_ge(b_ok, 1)

                        def exps(h, u):
                            j, t, b = u // NT, u % NT, u % 2
                            nw, nk = keys(t)
                            a.wait_ge(neg_ok, UNITS * h + u + 1)
                            a.activation(prob[b][:, 0:nk], S[b][:, 0:nk], ACT.Exp, bias=small[:, b, 2:3],
                                         accum_out=sums[:, u:u + 1]).then_inc(exp_ok, 1)

                        def evac(h, hp, s, n):
                            if 3 <= s < 6:
                                return
                            a.wait_ge(w_ps, n + 1)
                            a.sem_inc(a_passed, 1)
                            c, w = PIECES[s % 3]
                            if s < 3:
                                bias, dst = bq[:, 0, bass.ds(h, 1)], qT[hp][:, c:c + w]
                                how = dict(func=ACT.Identity, bias=bias, scale=HD ** -0.5)
                            elif s < QKV:
                                a.activation(flat(V[hp][:, :, :])[:, c:c + w], W[:, 0:w], ACT.Copy).then_inc(w_used, 1)
                                return
                            else:
                                dst = OT[:, bass.ds(h, 1), :].rearrange("p o n -> p (o n)")[:, c:c + w]
                                how = dict(func=ACT.Identity, bias=bq[:, 2, bass.ds(h, 1)])
                            if c + w > L:
                                a.activation(dst, W[:, 0:w], **how).then_inc(w_used, 1)
                            elif s < 3:
                                a.activation(rows_reversed(dst, w // GRID_W), W[:, 0:w].rearrange("p (r c) -> p r c", c=GRID_W),
                                             **how).then_inc(w_used, 1)
                            else:
                                a.activation(dst.rearrange("p (r c) -> p r c", c=GRID_W), rows_reversed(W[:, 0:w], w // GRID_W),
                                             **how).then_inc(w_used, 1)

                        def pair(h, hp, last):
                            at = {u: (s, n) for u, s, n in uses(h, last)}

                            def evac_at(u):
                                if u in at:
                                    s, n = at[u]
                                    mine = s >= QKV
                                    evac(h if mine else h + 1, hp if mine else 1 - hp, s, n)

                            exps(h, 0)
                            exps(h, 1)
                            for u in range(UNITS):
                                b = u % 2
                                nk = keys(u % NT)[1]
                                half = nk // P // 2 * P
                                a.wait_ge(pt_ok, UNITS * h + u + 1)
                                a.activation(probT[b][:, 0:half], PT[:, 0:half], ACT.Copy).then_inc(pa_ok, 1)
                                if u + 2 < UNITS:
                                    exps(h, u + 2)
                                evac_at(u)
                            evac_at(UNITS)

                        for s in range(QKV):
                            evac(0, 0, s, s)
                        turns(a, pair)

                    @block.vector
                    def _(v):
                        v.wait_ge(b_in, 16)

                        def softmax(h, u, link):
                            j, t, b = u // NT, u % NT, u % 2
                            nw, nk = keys(t)
                            v.wait_ge(s_ok, UNITS * h + u + 1)
                            link(v.reduce_max(small[:, b, 0:1], S[b][:, nw:nk], AX))
                            mx = small[:, b, 0:1]
                            if nw:
                                if u % NT == 0:
                                    v.wait_ge(bt_ok, 2 * h + j + 1)
                                r0 = window(t)[2]
                                v.sem_inc(v_passed, 1)
                                link(v.tensor_tensor_reduce(S[b][:, 0:nw], S[b][:, 0:nw], flat(tab[j][:, r0:r0 + nw // GRID_W, :]),
                                                            1.0, mx, ALU.add, ALU.max, small[:, b, 1:2]))
                                mx = small[:, b, 1:2]
                            v.tensor_scalar(small[:, b, 2:3], mx, -1.0, None, ALU.mult).then_inc(neg_ok, 1)

                        def evac(h, hp, s, n):
                            if 3 <= s < 6:
                                c, w = PIECES[s % 3]
                                v.wait_ge(w_ps, n + 1)
                                v.tensor_scalar(kT[hp][:, c:c + w], W[:, 0:w], bq[:, 1, bass.ds(h, 1)], None, ALU.add).then_inc(w_used, 1)

                        def pair(h, hp, last):
                            at = {u: (s, n) for u, s, n in uses(h, last)}
                            link = Chain(v, dv, 2 * (2 * NTL + NTC) + UNITS, h)
                            softmax(h, 0, link)
                            softmax(h, 1, link)
                            for u in range(UNITS):
                                j, t, b = u // NT, u % NT, u % 2
                                nk = keys(t)[1]
                                half = nk // P // 2 * P
                                v.wait_ge(pt_ok, UNITS * h + u + 1)
                                v.tensor_copy(probT[b][:, half:nk], PT[:, 512:512 + nk - half]).then_inc(pd_ok, 1)
                                if u + 2 < UNITS:
                                    softmax(h, u + 2, link)
                                if u in at:
                                    evac(h + 1, 1 - hp, *at[u])
                                v.wait_ge(exp_ok, UNITS * h + u + 1)
                                link(v.reciprocal(small[:, b, 3:4], sums[:, u:u + 1]))
                                v.wait_ge(o_ok, UNITS * h + u + 1)
                                v.tensor_scalar(osb[:, t, j * HD:(j + 1) * HD], O[:, 0:HD],
                                                small[:, b, 3:4], None, ALU.mult).then_inc(on_ok, 1)
                            link.end()

                        v.sem_inc(on_ok, 1)
                        for s in range(QKV):
                            evac(0, 0, s, s)
                        turns(v, pair)

                    @block.tensor
                    def _(t_):
                        pe = t_

                        def scores(h, hp, u):
                            j, t, b = u // NT, u % NT, u % 2
                            nw, nk = keys(t)
                            q = qT[hp][j * HD:(j + 1) * HD, t * P:(t + 1) * P]
                            k = kT[hp][j * HD:(j + 1) * HD, :]
                            if nw:
                                k0 = window(t)[0] * GRID_W
                                pe.matmul(S[b][:, 0:512], q, k[:, k0:k0 + 512], start=True, stop=True)
                                if nw > 512:
                                    pe.matmul(S[b][:, 512:nw], q, k[:, k0 + 512:k0 + nw], start=True, stop=True)
                            pe.matmul(S[b][:, nw:nk], q, k[:, L:N], start=True, stop=True).then_inc(s_ok, 1)

                        def use(h, s, n, first=False):
                            if not first:
                                pe.wait_ge(w_used, n)
                            c, w = PIECES[s % 3]
                            if s < QKV and s % 3 == 0:
                                pe.wait_ge(sl_in[s // 3], 16 * h + 16)
                            if s < 6:
                                for k in range(KD):
                                    mm = pe.matmul(W[:, 0:w], slab[s // 3][:, k, :], hT[:, k, c:c + w],
                                                   start=(k == 0), stop=(k == KD - 1))
                            elif s < QKV:
                                for t in range(w // P):
                                    for k in range(KD):
                                        mm = pe.matmul(W[:, t * P:(t + 1) * P], hT[:, k, c + t * P:c + (t + 1) * P],
                                                       slab[2][:, k, :], start=(k == 0), stop=(k == KD - 1))
                            else:
                                for t in range(w // P):
                                    mm = pe.transpose(W[:, t * P:(t + 1) * P], osb[:, c // P + t, :], ident[:, :])
                            mm.then_inc(w_ps, 1)

                        def pair(h, hp, last):
                            at = {u: (s, n) for u, s, n in uses(h, last)}
                            scores(h, hp, 0)
                            scores(h, hp, 1)
                            for u in range(UNITS):
                                j, t, b = u // NT, u % NT, u % 2
                                nw, nk = keys(t)
                                nc_ = nk // P
                                pe.wait_ge(exp_ok, UNITS * h + u + 1)
                                for c in range(nc_):
                                    to = c * P if c < nc_ // 2 else 512 + (c - nc_ // 2) * P
                                    mm = pe.transpose(PT[:, to:to + P], prob[b][:, c * P:(c + 1) * P], ident[:, :])
                                mm.then_inc(pt_ok, 1)
                                if u + 2 < UNITS:
                                    scores(h, hp, u + 2)
                                if u in at:
                                    use(h + 1, *at[u])
                                pe.wait_ge(pa_ok, UNITS * h + u + 1)
                                pe.wait_ge(pd_ok, UNITS * h + u + 1)
                                pe.wait_ge(on_ok, UNITS * h + u + 1)
                                tiles = [window(t)[0] // 2 + c for c in range(nw // P)] + [NTL, NTL + 1]
                                for c, kt in enumerate(tiles):
                                    mm = pe.matmul(O[:, 0:HD], probT[b][:, c * P:(c + 1) * P],
                                                   V[hp][:, kt, j * HD:(j + 1) * HD], start=(c == 0), stop=(c == nc_ - 1))
                                mm.then_inc(o_ok, 1)
                            pe.wait_ge(on_ok, UNITS * h + UNITS + 1)
                            use(h, *at[UNITS])

                        for s in range(QKV):
                            use(0, s, s, first=(s == 0))
                        pe.wait_ge(w_used, QKV)
                        turns(pe, pair)
        def projection(l, nt, Z, w_o, b_o, RL):
            n_pairs = nt // 2
            with ExitStack() as st:
                wo = sbuf(st, f"wo{l}", [P, KD, D])
                wr = sbuf(st, f"wr{l}", [P, KD, NR])
                rbias = sbuf(st, f"rbias{l}", [P, NR])
                ng, bo = sbuf(st, f"ng_p{l}", [P, D]), sbuf(st, f"bo{l}", [P, D])
                bg = sbuf(st, f"bg{l}", [P, 2, D])
                xt = [sbuf(st, f"xt_p{l}{j}", [P, D]) for j in range(2)]
                x1 = [sbuf(st, f"x1_p{l}{j}", [P, D]) for j in range(2)]
                hb = [sbuf(st, f"hb_p{l}{j}", [P, D]) for j in range(2)]
                ht = [sbuf(st, f"ht_p{l}{j}", [P, KD, P]) for j in range(2)]
                junk = sbuf(st, f"junk_p{l}", [P, D])
                ss, rt = sbuf(st, f"ss_p{l}", [P, 2]), sbuf(st, f"rt_p{l}", [P, 2])
                nm = lambda s: sem(f"{s}_p{l}")
                wo_in = [nm(f"wo_in{h}") for h in range(2)]
                wr_in, rows_in, rows_ok, bg_ok = nm("wr_in"), nm("rows"), nm("gain"), nm("bg")
                x_in = [nm(f"x_in{j}") for j in range(2)]
                x_out = [nm(f"x1_out{j}") for j in range(2)]
                h_out = [nm(f"h_out{j}") for j in range(2)]
                xb_ok, op_ok, x1_ok, sum_ok, sqrt_ok, h_ok = nm("xb"), nm("op"), nm("x1"), nm("sum"), nm("sqrt"), nm("h")
                tr_ok, ev_ok, rt_ok, rl_ok, dv = nm("tr"), nm("ev"), nm("router"), nm("rl"), nm("dve")

                with nc.Block() as block:
                    @block.sync
                    def _(sp):
                        for h in range(2):
                            half = slice(h * 512, (h + 1) * 512)
                            sp.dma_start(wo[:, :, half], w_o.rearrange("(k p) n -> p k n", p=P)[:, :, half]).then_inc(wo_in[h], 16)
                        load_gate(sp, rows_in, l, 0)
                        sp.dma_start(bo[:, :], row_to_all(b_o, D)).then_inc(rows_in, 16)

                        def load_x(j, src):
                            sp.dma_start(xt[j][:, :], src).then_inc(x_in[j], 16)

                        def source(n, i, j):
                            if l:
                                return x2_d[bass.ds((2 * i + j) * P, P), :]
                            return A["x"][0, bass.ds((2 * i + j) * P, P), :]

                        for j in range(2):
                            load_x(j, x2_d[j * P:(j + 1) * P, :] if l else A["x"][0, j * P:(j + 1) * P, :])
                        load_rows(sp, rows_in, l, 1, A["norm_g"][l, 1, :], ng[:, :])
                        sp.dma_start(rbias[:, 0:GROUPS], row_to_all(A["moe_b_group"][l, :], GROUPS)).then_inc(wr_in, 16)
                        sp.dma_start(rbias[:, GROUPS:NR], row_to_all(A["moe_b_expert"][l, 0, :], EXPERTS)).then_inc(wr_in, 16)
                        sp.dma_start(wr[:, :, 0:GROUPS], A["moe_w_group"][l].rearrange("(k p) g -> p k g", p=P)).then_inc(wr_in, 16)
                        for g in range(GROUPS):
                            sp.dma_start(wr[:, :, GROUPS + g * EPG:GROUPS + (g + 1) * EPG],
                                         A["moe_w_expert"][l, g].rearrange("(k p) e -> p k e", p=P)).then_inc(wr_in, 16)
                        with sp.Fori(1, NTL // 2) as i:
                            for j in range(2):
                                sp.wait_ge(x1_ok, 2 * i + j - 1)
                                load_x(j, source(None, i, j))
                        if nt > NTL:
                            for j in range(2):
                                sp.wait_ge(x1_ok, NTL + j - 1)
                                load_x(j, A["ctx"][0, j * P:(j + 1) * P, :])

                    @block.gpsimd
                    def _(g):
                        def bias(n, j, w):
                            g.wait_ge(x_in[j], (n - j) * 8 + 16)
                            g.tensor_tensor(xt[j][:, :], xt[j][:, :], bg[:, w, :], ALU.add).then_inc(xb_ok, 1)

                        g.wait_ge(bg_ok, 2)
                        with g.Fori(0, NTL // 2) as i:
                            for j in range(2):
                                bias(2 * i + j, j, 0)
                        if nt > NTL:
                            bias(NTL, 0, 1)
                            bias(NTL + 1, 1, 1)

                    @block.vector
                    def _(v):
                        v.wait_ge(rows_in, 128)
                        gain(v, ng[:, :], rows_ok)
                        for w in range(2):
                            v.tensor_tensor(bg[:, w, :], gt_rows[:, w, :], bo[:, :], ALU.mult).then_inc(bg_ok, 1)
                        v.wait_ge(bg_ok, 2)
                        v.wait_ge(wr_in, 16 * 7)

                        def tile(n, j, w, first=False):
                            link = Chain(v, dv, 4, n)
                            v.wait_ge(op_ok, n + 1)
                            if not first:
                                v.wait_ge(x_out[j], (n - j) * 8)
                            link(v.tensor_tensor(x1[j][:, :], banks(2 * j, 2), gt_rows[:, w, :], ALU.mult))
                            v.wait_ge(xb_ok, n + 1)
                            v.tensor_tensor(x1[j][:, :], x1[j][:, :], xt[j][:, :], ALU.add).then_inc(x1_ok, 1)
                            v.wait_ge(x1_ok, n + 1)
                            link(v.tensor_tensor_reduce(junk[:, :], x1[j][:, :], x1[j][:, :], 1.0 / D, 0.0, ALU.mult, ALU.add,
                                                        ss[:, j:j + 1]))
                            v.sem_inc(sum_ok, 1)
                            v.wait_ge(sqrt_ok, n + 1)
                            link(v.reciprocal(ss[:, j:j + 1], rt[:, j:j + 1]))
                            if not first:
                                v.wait_ge(tr_ok, n - 1)
                                v.wait_ge(h_out[j], (n - j) * 8)
                            link(v.scalar_tensor_tensor(out=hb[j][:, :], in0=x1[j][:, :], scalar=ss[:, j:j + 1],
                                                        in1=g_rows[:, w, :], op0=ALU.mult, op1=ALU.mult))
                            v.tensor_tensor(hb[j][:, :], hb[j][:, :], sh_rows[:, w, :], ALU.add).then_inc(h_ok, 1)
                            link.end()

                        def logits(n):
                            v.wait_ge(rt_ok, n + 1)
                            dst = RL[:, bass.ds(n, 1), :].rearrange("p o n -> p (o n)")
                            v.tensor_tensor(dst, PS[:, 6, 0:NR], rbias[:, :], ALU.add).then_inc(rl_ok, 1)

                        tile(0, 0, 0, True)
                        tile(1, 1, 0, True)
                        logits(0)
                        with v.Fori(1, NTL // 2) as i:
                            tile(2 * i, 0, 0)
                            logits(2 * i - 1)
                            tile(2 * i + 1, 1, 0)
                            logits(2 * i)
                        for n in range(NTL, nt):
                            tile(n, n % 2, 1)
                            logits(n - 1)
                        logits(nt - 1)

                    @block.scalar
                    def _(a):
                        def tile(n, j, rows, first=False):
                            a.wait_ge(x1_ok, n + 1)
                            a.dma_start(x1_d[rows, :], x1[j][:, :]).then_inc(x_out[j], 16)
                            a.wait_ge(sum_ok, n + 1)
                            if not first:
                                a.wait_ge(dv, 4 * (n - 2) + 3)
                            a.activation(rt[:, j:j + 1], ss[:, j:j + 1], ACT.Sqrt, bias=epst[:, :]).then_inc(sqrt_ok, 1)
                            a.wait_ge(h_ok, n + 1)
                            a.dma_start(h2_d[rows, :], hb[j][:, :]).then_inc(h_out[j], 16)

                        def evac(n, j, first=False):
                            a.wait_ge(tr_ok, n + 1)
                            if not first:
                                a.wait_ge(rt_ok, n - 1)
                            a.activation(flat(ht[j][:, :, :]), banks(4, 2), ACT.Copy).then_inc(ev_ok, 1)

                        tile(0, 0, slice(0, P), True)
                        evac(0, 0, True)
                        tile(1, 1, slice(P, 2 * P), True)
                        evac(1, 1, True)
                        with a.Fori(1, nt // 2) as i:
                            for j in range(2):
                                tile(2 * i + j, j, bass.ds((2 * i + j) * P, P))
                                evac(2 * i + j, j)
                        for j in range(2):
                            a.wait_ge(x_out[j], 8 * nt)
                            a.wait_ge(h_out[j], 8 * nt)

                    @block.tensor
                    def _(t):
                        def product(n):
                            if n >= 2:
                                t.wait_ge(x1_ok, n - 1)
                            for h in range(2):
                                if n == 0:
                                    t.wait_ge(wo_in[h], 16)
                                for k in range(KD):
                                    mm = t.matmul(PS[:, 2 * (n % 2) + h, :], Z[:, k, n * P:(n + 1) * P],
                                                  wo[:, k, h * 512:(h + 1) * 512], start=(k == 0), stop=(k == KD - 1))
                            mm.then_inc(op_ok, 1)

                        def route(n):
                            t.wait_ge(ev_ok, n + 1)
                            if n >= 1:
                                t.wait_ge(rl_ok, n)
                            for k in range(KD):
                                mm = t.matmul(PS[:, 6, 0:NR], ht[n % 2][:, k, :], wr[:, k, :], start=(k == 0), stop=(k == KD - 1))
                            mm.then_inc(rt_ok, 1)

                        product(0)
                        t.wait_ge(wr_in, 16 * 7)
                        for n in range(nt):
                            if n + 1 < nt:
                                product(n + 1)
                            if n:
                                route(n - 1)
                            transposes(t, n, n % 2, hb, h_ok, 4, ev_ok, tr_ok)
                        route(nt - 1)

        def routing(l, nt, RL, tabs, ng):
            dst, w01, item, item_slots, n_pairs = tabs
            with ExitStack() as st:
                T = lambda name, shape, dt=F32: sbuf(st, f"{name}_r{l}", [P] + shape, dt)
                io8i, ioti, toki, zi = T("io8i", [EPG], I32), T("ioti", [ITEMS], I32), T("toki", [NT], I32), T("zi", [ITEMS], I32)
                io8, iot = T("io8", [EPG]), T("iot", [ITEMS])
                gl, el, m4 = T("gl", [nt, GROUPS]), T("el", [nt, GROUPS, EPG]), T("m4", [nt, GROUPS])
                e8, m8, oh0, oh1 = T("e8", [nt, EPG]), T("m8", [nt, EPG]), T("oh0", [nt, EPG]), T("oh1", [nt, EPG])
                gmax, gsum, best, v0, v1 = (T(x, [nt]) for x in ("gmax", "gsum", "best", "v0", "v1"))
                goh = T("goh", [nt, GROUPS])
                OH = [T(f"OH{k}", [nt, EXPERTS]) for k in range(2)]
                A2, pre, cnt, run = T("A2", [nt, EXPERTS]), T("pre", [nt, EXPERTS]), T("cnt", [nt, EXPERTS]), T("run", [EXPERTS])
                blk, incl, base, one32 = T("blk", [EXPERTS]), T("incl", [EXPERTS]), T("base", [EXPERTS]), T("one32", [EXPERTS])
                NBLK = nt + 1
                cmpb, cmpi = T("cmpb", [EXPERTS, NBLK]), T("cmpi", [ITEMS, EXPERTS])
                itf, npf, cmpn = T("itf", [ITEMS]), T("npf", [1]), T("cmpn", [ITEMS // 2])
                df, dq, hi, adr = T("df", [2, nt]), T("dq", [2, nt]), T("hi", [2, nt]), T("adr", [2, nt], I32)
                cmph = T("cmph", [2 * nt, ITEMS - 1])
                prod = T("prod", [nt, EXPERTS])
                nm = lambda s: sem(f"{s}_r{l}")
                io_ok, dv, d_ok, e_ok, a_ok, cn_ok = nm("iota"), nm("dve"), nm("diff"), nm("exp"), nm("assigned"), nm("counts")
                rows_in, z_ok, ad_ok, sc_ok, sl_ok = nm("rows"), nm("zeroed"), nm("slots"), gather_sem(f"scattered_r{l}"), nm("loaded")
                with nc.Block() as block:
                    @block.gpsimd
                    def _(g):
                        g.memset(zi[:, :], 0).then_inc(io_ok, 1)
                        g.iota(io8i[:, :], pattern=[[-1, EPG]], base=EPG, channel_multiplier=0).then_inc(io_ok, 1)
                        g.iota(ioti[:, :], pattern=[[1, ITEMS]], base=0, channel_multiplier=0).then_inc(io_ok, 1)
                        g.iota(toki[:, :], pattern=[[P, NT]], base=0, channel_multiplier=1).then_inc(io_ok, 1)
                        g.wait_ge(io_ok, 4)
                        g.wait_ge(z_ok, 16)
                        g.wait_ge(ad_ok, 1)
                        for k in range(2):
                            for t in range(nt):
                                g.indirect_dma_start(out=slot_d[l][:, :], in_=toki[:, t:t + 1], in_offset=None,
                                                     out_offset=bass.IndirectOffsetOnAxis(ap=adr[:, k, t:t + 1], axis=0)
                                                     ).then_inc(sc_ok, 16)

                    @block.sync
                    def _(sp):
                        sp.wait_ge(io_ok, 4)
                        sp.dma_start(slot_d[l].rearrange("(p i) o -> p (i o)", p=P), zi[:, :]).then_inc(z_ok, 16)
                        load_gate(sp, rows_in, l, 1)
                        if l == 1:
                            sp.dma_start(ng[:, :], row_to_all(A["final_g"], D)).then_inc(rows_in, 16)
                        else:
                            load_rows(sp, rows_in, l + 1, 0, A["norm_g"][l + 1, 0, :], ng[:, :])
                        sp.wait_ge(sc_ok, 2 * nt * 16)
                        sp.dma_start(item_slots[:, :], slot_d[l].rearrange("(p i) o -> p (i o)", p=P)).then_inc(sl_ok, 16)
                        sp.wait_ge(sl_ok, 16)
                        sp.wait_ge(rows_in, 48 if l == 1 else 112)

                    @block.scalar
                    def _(a):
                        a.wait_ge(d_ok, 1)
                        a.activation(flat(m4[:, :, :]), flat(gl[:, :, :]), ACT.Exp).then_inc(e_ok, 1)
                        a.wait_ge(d_ok, 2)
                        a.activation(v1[:, :], v1[:, :], ACT.Exp).then_inc(e_ok, 1)

                    @block.tensor
                    def _(t):
                        t.wait_ge(a_ok, 1)
                        t.matmul(PS[:, 0, 0:nt * EXPERTS], ltri[:, :], flat(A2[:, :, :]), start=True, stop=True)
                        t.matmul(PS[:, 1, 0:nt * EXPERTS], ones[:, :], flat(A2[:, :, :]), start=True, stop=True).then_inc(cn_ok, 1)

                    @block.vector
                    def _(v):
                        n = [0]

                        def link(ins):
                            n[0] += 1
                            ins.then_inc(dv, 1)
                            v.wait_ge(dv, n[0])

                        def first_best(val, mx, mask, hot, width):
                            link(v.tensor_reduce(mx[:, :], val[:, :, :], AX, ALU.max))
                            link(v.tensor_tensor(mask[:, :, :], val[:, :, :], expand(mx[:, :], (2, width)), ALU.is_equal))
                            link(v.tensor_tensor(mask[:, :, :], mask[:, :, :], expand(io8[:, 0:width], (1, nt)), ALU.mult))
                            link(v.tensor_reduce(best[:, :], mask[:, :, :], AX, ALU.max))
                            link(v.tensor_tensor(hot[:, :, :], mask[:, :, :], expand(best[:, :], (2, width)), ALU.is_equal))

                        v.wait_ge(io_ok, 4)
                        link(v.tensor_copy(io8[:, :], io8i[:, :]))
                        link(v.tensor_copy(iot[:, :], ioti[:, :]))
                        link(v.memset(one32[:, :], 1.0))
                        link(v.tensor_copy(gl[:, :, :], RL[:, 0:nt, 0:GROUPS]))
                        first_best(gl, gmax, m4, goh, GROUPS)
                        v.tensor_tensor(gl[:, :, :], gl[:, :, :], expand(gmax[:, :], (2, GROUPS)), ALU.subtract).then_inc(d_ok, 1)
                        rle = RL[:, 0:nt, GROUPS:NR].rearrange("p t (g e) -> p t g e", g=GROUPS)
                        link(v.tensor_tensor(el[:, :, :, :], rle, expand(goh[:, :, :], (3, EPG)), ALU.mult))
                        link(v.tensor_reduce(e8[:, :, :], el[:, :, :, :].rearrange("p t g e -> p t e g"), AX, ALU.add))
                        first_best(e8, v0, m8, oh0, EPG)
                        link(v.tensor_scalar(m8[:, :, :], oh0[:, :, :], NEG, None, ALU.mult))
                        link(v.tensor_tensor(e8[:, :, :], e8[:, :, :], m8[:, :, :], ALU.add))
                        first_best(e8, v1, m8, oh1, EPG)
                        v.tensor_tensor(v1[:, :], v1[:, :], v0[:, :], ALU.subtract).then_inc(d_ok, 1)
                        v.wait_ge(e_ok, 2)
                        link(v.tensor_reduce(gsum[:, :], m4[:, :, :], AX, ALU.add))
                        link(v.tensor_scalar(v0[:, :], v1[:, :], 1.0, None, ALU.add))
                        link(v.tensor_tensor(v0[:, :], v0[:, :], gsum[:, :], ALU.mult))
                        link(v.reciprocal(w01[:, 0, :], v0[:, :]))
                        link(v.tensor_tensor(w01[:, 1, :], w01[:, 0, :], v1[:, :], ALU.mult))
                        for k, oh in enumerate((oh0, oh1)):
                            link(v.tensor_tensor(OH[k][:, :, :].rearrange("p t (g e) -> p t g e", g=GROUPS),
                                                 expand(goh[:, :, :], (3, EPG)), expand(oh[:, :, :], (2, GROUPS)), ALU.mult))
                        v.tensor_tensor(A2[:, :, :], OH[0][:, :, :], OH[1][:, :, :], ALU.add).then_inc(a_ok, 1)
                        v.wait_ge(cn_ok, 1)
                        link(v.tensor_copy(flat(pre[:, :, :]), PS[:, 0, 0:nt * EXPERTS]))
                        link(v.tensor_copy(flat(cnt[:, :, :]), PS[:, 1, 0:nt * EXPERTS]))
                        link(v.tensor_copy(run[:, :], cnt[:, 0, :]))
                        for t in range(1, nt):
                            link(v.tensor_tensor(pre[:, t, :], pre[:, t, :], run[:, :], ALU.add))
                            link(v.tensor_tensor(run[:, :], run[:, :], cnt[:, t, :], ALU.add))
                        link(v.tensor_scalar(run[:, :], run[:, :], 1.0 / P, None, ALU.mult))
                        link(v.tensor_tensor(cmpb[:, :, :], expand(run[:, :], (2, NBLK)), expand(iot[:, 0:NBLK], (1, EXPERTS)), ALU.is_gt))
                        link(v.tensor_reduce(blk[:, :], cmpb[:, :, :], AX, ALU.add))
                        link(v.tensor_tensor_scan(incl[:, :], one32[:, :], blk[:, :], 0.0, ALU.mult, ALU.add))
                        link(v.tensor_tensor(base[:, :], incl[:, :], blk[:, :], ALU.subtract))
                        link(v.tensor_scalar(base[:, :], base[:, :], float(P), None, ALU.mult))
                        link(v.tensor_tensor(pre[:, :, :], pre[:, :, :], expand(base[:, :], (1, nt)), ALU.add))
                        for k in range(2):
                            link(v.tensor_tensor(prod[:, :, :], pre[:, :, :], OH[k][:, :, :], ALU.mult))
                            link(v.tensor_reduce(df[:, k, :], prod[:, :, :], AX, ALU.add))
                        link(v.tensor_copy(flat(dst[:, :, :]), flat(df[:, :, :])))
                        link(v.tensor_scalar(flat(dq[:, :, :]), flat(df[:, :, :]), 1.0 / P, None, ALU.mult))
                        link(v.tensor_tensor(cmph[:, :, :], expand(flat(dq[:, :, :]), (2, ITEMS - 1)),
                                             expand(iot[:, 1:ITEMS], (1, 2 * nt)), ALU.is_ge))
                        link(v.tensor_reduce(flat(hi[:, :, :]), cmph[:, :, :], AX, ALU.add))
                        link(v.tensor_scalar(flat(hi[:, :, :]), flat(hi[:, :, :]), -(P * ITEMS - 1.0), None, ALU.mult))
                        link(v.scalar_tensor_tensor(out=flat(hi[:, :, :]), in0=flat(df[:, :, :]), scalar=float(ITEMS),
                                                    in1=flat(hi[:, :, :]), op0=ALU.mult, op1=ALU.add))
                        v.tensor_copy(flat(adr[:, :, :]), flat(hi[:, :, :])).then_inc(ad_ok, 1)
                        link(v.tensor_tensor(cmpi[:, :, :], expand(iot[:, :], (2, EXPERTS)), expand(incl[:, :], (1, ITEMS)), ALU.is_ge))
                        link(v.tensor_reduce(itf[:, :], cmpi[:, :, :], AX, ALU.add))
                        link(v.tensor_scalar(itf[:, :], itf[:, :], EXPERTS - 1.0, None, ALU.min))
                        link(v.tensor_copy(item[:, :], itf[:, :]))
                        link(v.tensor_scalar(cmpn[:, :], iot[:, 0:ITEMS:2], incl[:, EXPERTS - 1:EXPERTS], None, ALU.is_lt))
                        link(v.tensor_reduce(npf[:, :], cmpn[:, :], AX, ALU.add))
                        link(v.tensor_copy(n_pairs[:, :], npf[:, :]))

        RAW, PARTS = 6, 4

        def experts(l, tabs):
            dst, w01, item, item_slots, n_pairs = tabs
            with ExitStack() as st:
                raw = [sbuf(st, f"raw_{l}{r}", [P, 4 * FF]) for r in range(RAW)]
                whi = [sbuf(st, f"whi_{l}{r}", [P, 4 * FF], F32R) for r in range(PARTS)]
                wlo = [sbuf(st, f"wlo_{l}{r}", [P, 4 * FF], F32R) for r in range(PARTS)]
                ib = [sbuf(st, f"ib_{l}{j}", [P, 1], I32) for j in range(2)]
                xg = [sbuf(st, f"xg_{l}{j}", [P, D]) for j in range(2)]
                xhi = [sbuf(st, f"xhi_{l}{j}", [P, D], F32R) for j in range(2)]
                xlo = [sbuf(st, f"xlo_{l}{j}", [P, D], F32R) for j in range(2)]
                th, u, hid = sbuf(st, f"th_{l}", [P, FF]), sbuf(st, f"u_{l}", [P, FF]), sbuf(st, f"hid_{l}", [P, FF])
                hhi, hlo = sbuf(st, f"hhi_{l}", [P, FF], F32R), sbuf(st, f"hlo_{l}", [P, FF], F32R)
                y = [sbuf(st, f"y_{l}{j}", [P, D]) for j in range(2)]
                nm = lambda s: sem(f"{s}_e{l}")
                raw_in = [nm(f"raw{r}") for r in range(RAW)]
                y_out = [nm(f"y_out{j}") for j in range(2)]
                g_in = [gather_sem(f"rows{j}_e{l}") for j in range(2)]
                hi_ok, lo_ok, share_used = nm("high"), nm("low"), nm("share_used")
                ib_ok, xt_ps, xh_ok, xl_ok = nm("ib"), nm("xT_ps"), nm("x_high"), nm("x_low")
                th_ok, u_ok, hid_ok = nm("tanh"), nm("u"), nm("hid")
                ht_ps, hh_ok, hl_ok, ya_ok = nm("hidT_ps"), nm("hid_high"), nm("hid_low"), nm("y")
                passed, a_passed, passed_sp = nm("passed"), nm("act_passed"), nm("sp_passed")
                w1v, w3v = (A[k][l].rearrange("e (s k p) f -> e s p k f", p=P, s=2) for k in ("moe_w1", "moe_w3"))
                w2v = A["moe_w2"][l].rearrange("e (s k p) d -> e s p k d", p=P, s=2)
                most = dict(min_val=1, max_val=(MAX_ITEMS + 1) // 2)
                W3A, W3B, W1A, W1B, W2A, W2B, W3C, W3D = range(2, 10)

                with nc.Block() as block:
                    @block.sync
                    def _(sp):
                        def load(n, q, view, e, s, k, first=False, kept=None):
                            if not first:
                                sp.wait_ge(lo_ok, 6 * n + q + 1)
                                sp.sem_inc(passed_sp, 1)
                            src = view[bass.ds(e, 1), s].rearrange("o p k f -> (o p) k f")
                            dst_ = raw[q % RAW][:, :].rearrange("p (k f) -> p k f", k=k)
                            if kept is None:
                                sp.dma_start(dst_, src).then_inc(raw_in[q % RAW], 16)
                                return
                            with sp.If(e != kept):
                                sp.dma_start(dst_, src).then_inc(raw_in[q % RAW], 16)
                            with sp.Else():
                                sp.sem_inc(raw_in[q % RAW], 16)

                        count = sp.value_load(n_pairs[0:1, 0:1], **most)
                        e0 = sp.value_load(item[0:1, 0:1], min_val=0, max_val=EXPERTS - 1)
                        for s in range(2):
                            load(0, s, w1v, e0, s, 4, True)
                        for s in range(2):
                            load(0, 2 + s, w3v, e0, s, 4, True)
                        with sp.Fori(0, count) as i:
                            for j in range(2):
                                n = 2 * i + j
                                e = sp.value_load(item[0:1, bass.ds(n, 1)], min_val=0, max_val=EXPERTS - 1)
                                e1 = sp.value_load(item[0:1, bass.ds(n + 1, 1)], min_val=0, max_val=EXPERTS - 1)
                                for s in range(2):
                                    load(n, W1A + s, w1v, e1, s, 4, kept=e)
                                for s in range(2):
                                    load(n, W2A + s, w2v, e, s, 2)
                                for s in range(2):
                                    load(n, W3C + s, w3v, e1, s, 4, kept=e)

                    @block.gpsimd
                    def _(g):
                        count = g.value_load(n_pairs[0:1, 0:1], **most)

                        def gather(n, j):
                            g.wait_ge(xt_ps, n + 1)
                            g.tensor_copy(ib[j][:, :], item_slots[:, bass.ds(n, 1)]).then_inc(ib_ok, 1)
                            g.wait_ge(ib_ok, n + 1)
                            g.sem_inc(passed, 1)
                            g.indirect_dma_start(out=xg[j][:, :], out_offset=None, in_=h2_d[:, :],
                                                 in_offset=bass.IndirectOffsetOnAxis(ap=ib[j][:, :], axis=0)).then_inc(g_in[j], 16)

                        gather(0, 0)
                        with g.Fori(0, count) as i:
                            gather(2 * i + 1, 1)
                            gather(2 * i + 2, 0)
                        g.wait_ge(g_in[0], count * 16 + 16)

                    @block.scalar
                    def _(a):
                        count = a.value_load(n_pairs[0:1, 0:1], **most)

                        def high(n, j, q):
                            a.wait_ge(raw_in[q % RAW], 16 * (n + q // RAW + 1))
                            a.wait_ge(share_used, 6 * n + q + 1)
                            a.activation(whi[(6 * j + q) % PARTS][:, :], raw[q % RAW][:, :], ACT.Copy).then_inc(hi_ok, 1)

                        def x_high(n, j):
                            a.wait_ge(xt_ps, n + 3)
                            a.activation(xhi[j][:, :], banks(0, 2), ACT.Copy).then_inc(xh_ok, 1)

                        def tanh(n, done):
                            a.wait_ge(share_used, done)
                            a.wait_ge(u_ok, n + 1)
                            a.activation(th[:, :], PS[:, 2, :], ACT.Tanh, scale=0.5).then_inc(th_ok, 1)

                        a.sem_inc(ya_ok, 1)
                        for j in range(2):
                            a.sem_inc(y_out[j], 16)
                        high(0, 0, 0)
                        high(0, 0, 1)
                        x_high(0, 0)
                        high(0, 0, 2)
                        high(0, 0, 3)
                        tanh(0, PARTS + 2)
                        with a.Fori(0, count) as i:
                            for j in range(2):
                                n = 2 * i + j
                                x_high(n + 1, 1 - j)
                                for q in (W1A, W1B, W2A, W2B):
                                    high(n, j, q)
                                a.wait_ge(ht_ps, n + 2)
                                a.activation(hhi[:, :], PS[:, 4, :], ACT.Copy).then_inc(hh_ok, 1)
                                tanh(n + 1, 6 * n + W1B + PARTS + 1)
                                high(n, j, W3C)
                                high(n, j, W3D)
                                a.wait_ge(share_used, 6 * n + W2B + PARTS + 1)
                                a.wait_ge(y_out[j], 16 * i + 16)
                                a.activation(y[j][:, :], banks(5, 2), ACT.Copy).then_inc(ya_ok, 1)
                                a.wait_ge(ya_ok, n + 2)
                                a.dma_start(ys_d[bass.ds(n * P, P), :], y[j][:, :]).then_inc(y_out[j], 16)
                        for j in range(2):
                            a.wait_ge(y_out[j], 16 * count + 16)
                        a.sem_inc(a_passed, 1)

                    @block.vector
                    def _(v):
                        count = v.value_load(n_pairs[0:1, 0:1], **most)

                        def low(n, j, q):
                            v.wait_ge(hi_ok, 6 * n + q + 1)
                            r = (6 * j + q) % PARTS
                            v.tensor_tensor(wlo[r][:, :], raw[q % RAW][:, :], whi[r][:, :].bitcast(F32), ALU.subtract).then_inc(lo_ok, 1)

                        def x_low(n, j):
                            v.wait_ge(xh_ok, n + 1)
                            v.tensor_tensor(xlo[j][:, :], banks(0, 2), xhi[j][:, :].bitcast(F32), ALU.subtract).then_inc(xl_ok, 1)

                        def half_silu(n):
                            v.wait_ge(th_ok, n + 1)
                            v.wait_ge(hid_ok, n + 1)
                            v.scalar_tensor_tensor(out=u[:, :], in0=th[:, :], scalar=1.0, in1=PS[:, 2, :],
                                                   op0=ALU.add, op1=ALU.mult).then_inc(u_ok, 1)

                        v.sem_inc(lo_ok, RAW)
                        for s in (xl_ok, u_ok, hid_ok, hl_ok):
                            v.sem_inc(s, 1)
                        low(0, 0, 0)
                        low(0, 0, 1)
                        x_low(0, 0)
                        low(0, 0, 2)
                        low(0, 0, 3)
                        half_silu(0)
                        with v.Fori(0, count) as i:
                            for j in range(2):
                                n = 2 * i + j
                                x_low(n + 1, 1 - j)
                                low(n, j, W1A)
                                low(n, j, W1B)
                                v.wait_ge(share_used, 6 * n + W3B + PARTS + 1)
                                v.wait_ge(ht_ps, n + 1)
                                v.wait_ge(u_ok, n + 2)
                                v.scalar_tensor_tensor(out=hid[:, :], in0=u[:, :], scalar=0.5, in1=PS[:, 3, :],
                                                       op0=ALU.mult, op1=ALU.mult).then_inc(hid_ok, 1)
                                low(n, j, W2A)
                                low(n, j, W2B)
                                v.wait_ge(hh_ok, n + 1)
                                v.tensor_tensor(hlo[:, :], PS[:, 4, :], hhi[:, :].bitcast(F32), ALU.subtract).then_inc(hl_ok, 1)
                                half_silu(n + 1)
                                low(n, j, W3C)
                                low(n, j, W3D)

                    @block.tensor
                    def _(t):
                        count = t.value_load(n_pairs[0:1, 0:1], **most)
                        t.sem_inc(share_used, PARTS)
                        t.sem_inc(xt_ps, 2)
                        t.sem_inc(ht_ps, 1)

                        def rows_T(n, j, half):
                            t.wait_ge(g_in[j], half * 16 + 16)
                            t.wait_ge(xl_ok, n + 1)
                            for k in range(KD):
                                mm = t.transpose(banks(0, 2)[:, k * P:(k + 1) * P], xg[j][:, k * P:(k + 1) * P], ident[:, :])
                            mm.then_inc(xt_ps, 1)

                        def up(n, j, q, jx, bank, s):
                            t.wait_ge(lo_ok, 6 * n + q + RAW + 1)
                            r = (6 * j + q) % PARTS
                            for k in range(4):
                                c = (4 * s + k) * P
                                mm = three(t, PS[:, bank, :], xhi[jx][:, c:c + P], xlo[jx][:, c:c + P],
                                           whi[r][:, k * FF:(k + 1) * FF], wlo[r][:, k * FF:(k + 1) * FF],
                                           s == 0 and k == 0, s == 1 and k == 3)
                            mm.then_inc(share_used, 1)

                        rows_T(0, 0, 0)
                        t.wait_ge(xl_ok, 2)
                        up(0, 0, 0, 0, 2, 0)
                        up(0, 0, 1, 0, 2, 1)
                        with t.Fori(0, count) as i:
                            for j in range(2):
                                n = 2 * i + j
                                rows_T(n + 1, 1 - j, i + j)
                                t.wait_ge(hid_ok, n + 1)
                                up(n, j, W3A, j, 3, 0)
                                up(n, j, W3B, j, 3, 1)
                                t.wait_ge(xl_ok, n + 3)
                                t.wait_ge(u_ok, n + 2)
                                up(n, j, W1A, 1 - j, 2, 0)
                                t.wait_ge(hid_ok, n + 2)
                                t.wait_ge(hl_ok, n + 1)
                                for k in range(KF):
                                    mm = t.transpose(PS[:, 4, k * P:(k + 1) * P], hid[:, k * P:(k + 1) * P], ident[:, :])
                                mm.then_inc(ht_ps, 1)
                                up(n, j, W1B, 1 - j, 2, 1)
                                t.wait_ge(hl_ok, n + 2)
                                t.wait_ge(ya_ok, n + 1)
                                for s in range(2):
                                    t.wait_ge(lo_ok, 6 * n + W2A + s + RAW + 1)
                                    r = (6 * j + W2A + s) % PARTS
                                    for k in range(2):
                                        c = (2 * s + k) * P
                                        for h in range(2):
                                            w = slice(k * D + h * 512, k * D + (h + 1) * 512)
                                            mm = three(t, PS[:, 5 + h, :], hhi[:, c:c + P], hlo[:, c:c + P],
                                                       whi[r][:, w], wlo[r][:, w], s == 0 and k == 0, s == 1 and k == 1)
                                    mm.then_inc(share_used, 1)

        def combine(l, nt, tabs, ng, hT):
            dst, w01 = tabs[0], tabs[1]
            last = hT is None
            with ExitStack() as st:
                bufs = lambda name, shape, dt=F32: [sbuf(st, f"{name}_c{l}{j}", shape, dt) for j in range(2)]
                ib, wb = bufs("ib", [P, 2], I32), bufs("wb", [P, 2])
                y0, y1, xt, x2, hb = bufs("y0", [P, D]), bufs("y1", [P, D]), bufs("xt", [P, D]), bufs("x2", [P, D]), bufs("hb", [P, D])
                junk = sbuf(st, f"junk_c{l}", [P, D])
                ss, rt, rs = (sbuf(st, f"{x}_c{l}", [P, 2]) for x in ("ss", "rt", "rs"))
                nm = lambda s: sem(f"{s}_c{l}")
                x_in, x_out, h_out = ([nm(f"{s}{j}") for j in range(2)] for s in ("x_in", "x_out", "h_out"))
                y_in = [gather_sem(f"y_in{j}_c{l}") for j in range(2)]
                rows_ok, ib_ok, y_used, x2_ok = nm("gain"), nm("ib"), nm("y_used"), nm("x2")
                sum_ok, sqrt_ok, h_ok, tr_ok, ev_ok, dv, passed = (nm(s) for s in ("sum", "sqrt", "h", "tr", "ev", "dve", "passed"))
                norm_ok, rs_ok = nm("normed"), nm("rs")

                with nc.Block() as block:
                    @block.sync
                    def _(sp):
                        for j in range(2):
                            sp.dma_start(xt[j][:, :], x1_d[j * P:(j + 1) * P, :]).then_inc(x_in[j], 16)
                        with sp.Fori(1, nt // 2) as i:
                            for j in range(2):
                                sp.wait_ge(x2_ok, 2 * i + j - 1)
                                sp.dma_start(xt[j][:, :], x1_d[bass.ds((2 * i + j) * P, P), :]).then_inc(x_in[j], 16)

                    @block.gpsimd
                    def _(g):
                        def gather(n, j):
                            g.wait_ge(y_used, n + 1)
                            for k in range(2):
                                g.tensor_copy(ib[j][:, k:k + 1], dst[:, k, bass.ds(n, 1)]).then_inc(ib_ok, 1)
                            g.wait_ge(ib_ok, 2 * n + 2)
                            g.sem_inc(passed, 1)
                            for k, y in enumerate((y0, y1)):
                                g.indirect_dma_start(out=y[j][:, :], out_offset=None, in_=ys_d[:, :],
                                                     in_offset=bass.IndirectOffsetOnAxis(ap=ib[j][:, k:k + 1], axis=0)
                                                     ).then_inc(y_in[j], 16)

                        with g.Fori(0, nt // 2) as i:
                            for j in range(2):
                                gather(2 * i + j, j)

                    @block.vector
                    def _(v):
                        v.sem_inc(y_used, 2)
                        if not last:
                            gain(v, ng[:, :], rows_ok)

                        def add(n, j, w, first=False):
                            link = Chain(v, dv, 4, n)
                            for k in range(2):
                                link(v.tensor_copy(wb[j][:, k:k + 1], w01[:, k, bass.ds(n, 1)]))
                            v.wait_ge(y_in[j], (n - j) * 16 + 32)
                            link(v.tensor_scalar(y0[j][:, :], y0[j][:, :], wb[j][:, 0:1], None, ALU.mult))
                            link(v.scalar_tensor_tensor(out=y1[j][:, :], in0=y1[j][:, :], scalar=wb[j][:, 1:2], in1=y0[j][:, :],
                                                        op0=ALU.mult, op1=ALU.add))
                            if not first:
                                if not last:
                                    v.wait_ge(x_out[j], (n - j) * 8)
                            v.tensor_tensor(x2[j][:, :], y1[j][:, :], gt_rows[:, w, :], ALU.mult).then_inc(y_used, 1)
                            v.wait_ge(y_used, n + 3)
                            v.wait_ge(x_in[j], (n - j) * 8 + 16)
                            v.tensor_tensor(x2[j][:, :], x2[j][:, :], xt[j][:, :], ALU.add).then_inc(x2_ok, 1)
                            link.end()

                        def norm(n, j, w, first=False):
                            v.wait_ge(sqrt_ok, n + 1)
                            v.reciprocal(rs[:, j:j + 1], rt[:, j:j + 1]).then_inc(rs_ok, 1)
                            v.wait_ge(rs_ok, n + 1)
                            if not first:
                                if last:
                                    v.wait_ge(h_out[j], (n - j) * 8)
                                else:
                                    v.wait_ge(tr_ok, n - 1)
                            if last:
                                v.scalar_tensor_tensor(out=hb[j][:, :], in0=x2[j][:, :], scalar=rs[:, j:j + 1],
                                                       in1=ng[:, :], op0=ALU.mult, op1=ALU.mult).then_inc(h_ok, 1)
                            else:
                                v.scalar_tensor_tensor(out=hb[j][:, :], in0=x2[j][:, :], scalar=rs[:, j:j + 1],
                                                       in1=g_rows[:, w, :], op0=ALU.mult, op1=ALU.mult).then_inc(norm_ok, 1)
                                v.wait_ge(norm_ok, n + 1)
                                v.tensor_tensor(hb[j][:, :], hb[j][:, :], sh_rows[:, w, :], ALU.add).then_inc(h_ok, 1)

                        add(0, 0, 0, True)
                        add(1, 1, 0, True)
                        norm(0, 0, 0, True)
                        add(2, 0, 0)
                        norm(1, 1, 0, True)
                        with v.Fori(1, NTL // 2 - 1) as i:
                            add(2 * i + 1, 1, 0)
                            norm(2 * i, 0, 0)
                            add(2 * i + 2, 0, 0)
                            norm(2 * i + 1, 1, 0)
                        add(NTL - 1, 1, 0)
                        norm(NTL - 2, 0, 0)
                        for n in range(NTL, nt):
                            add(n, n % 2, 1)
                            norm(n - 1, (n - 1) % 2, 0 if n == NTL else 1)
                        norm(nt - 1, (nt - 1) % 2, 1 if nt > NTL else 0)

                    @block.scalar
                    def _(a):
                        def root_(n, j, first=False):
                            a.wait_ge(x2_ok, n + 1)
                            if not first:
                                a.wait_ge(sum_ok, n)
                            a.activation(junk[:, :], x2[j][:, :], ACT.Square, accum_out=ss[:, j:j + 1]).then_inc(sum_ok, 1)
                            a.wait_ge(sum_ok, n + 1)
                            if not first:
                                a.wait_ge(rs_ok, n - 1)
                            a.activation(rt[:, j:j + 1], ss[:, j:j + 1], ACT.Sqrt, bias=epst[:, :], scale=1.0 / D).then_inc(sqrt_ok, 1)

                        def tile(n, j, rows, first=False):
                            if not last:
                                a.wait_ge(x2_ok, n + 1)
                                a.dma_start(x2_d[rows, :], x2[j][:, :]).then_inc(x_out[j], 16)
                            root_(n, j, first)

                        def store(n, j, rows):
                            if last:
                                a.wait_ge(h_ok, n + 1)
                                a.dma_start(out[0, rows, :], hb[j][:, :]).then_inc(h_out[j], 16)

                        def evac(n, j):
                            if not last:
                                a.wait_ge(tr_ok, n + 1)
                                a.activation(hT[:, :, bass.ds(n * P, P)], banks(2 * j, 2).rearrange("p (k c) -> p k c", k=KD),
                                             ACT.Copy).then_inc(ev_ok, 1)

                        rows = lambda n: bass.ds(n * P, P)
                        tile(0, 0, slice(0, P), True)
                        tile(1, 1, slice(P, 2 * P), True)
                        store(0, 0, slice(0, P))
                        evac(0, 0)
                        with a.Fori(1, nt // 2) as i:
                            for j in range(2):
                                n = 2 * i + j
                                tile(n, j, rows(n))
                                store(n - 1, 1 - j, rows(n - 1))
                                evac(n - 1, 1 - j)
                        store(nt - 1, 1, slice((nt - 1) * P, nt * P))
                        evac(nt - 1, 1)
                        for j in range(2):
                            a.wait_ge(h_out[j] if last else x_out[j], 8 * nt)

                    if not last:
                        @block.tensor
                        def _(t):
                            t.sem_inc(ev_ok, 2)
                            with t.Fori(0, nt // 2) as i:
                                for j in range(2):
                                    n = 2 * i + j
                                    t.wait_ge(ev_ok, n + 1)
                                    transposes(t, n, j, hb, h_ok, 2 * j, ev_ok, tr_ok)

        def recurrent(hT, zT, yb):
            CW = 4
            UPW = N + 2 * (CW - 1)
            LAT0, CTX0 = 2, L + CW - 1 + 2
            CVW = L + CW - 1 + C
            with ExitStack() as st:
                wu, wy = sbuf(st, "wu", [P, KD, LBW]), sbuf(st, "wy", [P, KD, LBW])
                wg = sbuf(st, "wg", [P, 4, 2, LBW])
                UP = [sbuf(st, f"up{o}", [P, UPW]) for o in range(2)]
                uT = [sbuf(st, f"uT{o}", [P, N]) for o in range(2)]
                cv, tr = sbuf(st, "cv", [P, CVW]), sbuf(st, "tr", [P, N])
                ti, aa, qq, hh = ([sbuf(st, f"{s}{d}", [P, N]) for d in range(2)] for s in ("ti", "aa", "qq", "hh"))
                y2 = sbuf(st, "y2", [P, L])
                bin_, cw, cb = sbuf(st, "bin", [P, 2, KD]), sbuf(st, "cw", [P, CW, KD]), sbuf(st, "cb", [P, KD])
                bg = sbuf(st, "bgate", [P, 4, KD])
                lam, z_, s_, s2, acc = (sbuf(st, x, [P, 2, KD]) for x in ("lam", "lz", "ls", "ls2", "lacc"))
                c1, nc1 = sbuf(st, "c1", [P, 2, KD]), sbuf(st, "nc1", [P, 2, KD])
                wu_in, wy_in, wg_in, p_in = sem("wu_in"), sem("wy_in"), sem("wg_in"), sem("lru_p")
                e_in, e_ok, c_ok = sem("lam_abs"), sem("lam_exp"), sem("lru_c")
                u_ps, y_ps, r_ps, i_ps = sem("u_ps"), sem("y_ps"), sem("r_ps"), sem("i_ps")
                up_ok, pad_ok, u_ok = sem("up"), sem("pads"), sem("uT")
                tr_ok, ti_ok, a_ok, t2_ok, q_ok, sq_ok = (sem(x) for x in ("lr", "li", "la", "lt2", "lq", "lsq"))
                y_ok, y2_ok, gi_ok, gt_ok, z_ok = (sem(x) for x in ("yb", "y2", "gelu_in", "gelu_t", "z"))
                dv, hd_ok, c_once = sem("lru_dve"), sem("scanned"), sem("lru_once")
                sp_passed = sem("lru_sp_passed")
                wiv = A["lru_w_in"][0].rearrange("(k p) n -> p k n", p=P)
                wgv = A["lru_w_gate"][0].rearrange("d g b (c p) n -> b p (d g) c n", p=P)
                SA, SB = banks(0, 3), banks(3, 3)

                def back(ap):
                    n = ap.ap[-1][1]
                    return bass.AP(tensor=ap.tensor, offset=ap.offset + n - 1, ap=[list(ap.ap[0]), [-1, n]])

                with nc.Block() as block:
                    @block.sync
                    def _(sp):
                        def params():
                            sp.dma_start(lam[:, :, :], A["lru_lambda"][0].rearrange("d (k p) -> p d k", p=P)).then_inc(p_in, 16)
                            sp.dma_start(bin_[:, :, :], A["lru_b_in"][0].rearrange("(m k p) -> p m k", p=P, m=2)).then_inc(p_in, 16)
                            sp.dma_start(cw[:, :, :], A["lru_conv_w"][0].rearrange("w (k p) -> p w k", p=P)).then_inc(p_in, 16)
                            sp.dma_start(cb[:, :], A["lru_conv_b"][0].rearrange("(k p) -> p k", p=P)).then_inc(p_in, 16)
                            sp.dma_start(bg[:, :, :], A["lru_b_gate"][0].rearrange("d g (k p) -> p (d g) k", p=P)).then_inc(p_in, 16)

                        def load(b, first):
                            if not first:
                                sp.wait_ge(u_ps, 2 * b)
                                sp.sem_inc(sp_passed, 1)
                            sp.dma_start(wu[:, :, :], wiv[:, :, bass.ds(LW + b * LBW, LBW)]).then_inc(wu_in, 16)
                            if first:
                                params()
                            if not first:
                                sp.wait_ge(y_ps, 2 * b)
                                sp.sem_inc(sp_passed, 1)
                            sp.dma_start(wy[:, :, :], wiv[:, :, bass.ds(b * LBW, LBW)]).then_inc(wy_in, 16)
                            if not first:
                                sp.wait_ge(i_ps, 4 * b + 1)
                                sp.sem_inc(sp_passed, 1)
                            for q in range(4):
                                sp.dma_start(wg[:, q, :, :], wgv[bass.ds(b, 1), :, q, :, :].rearrange("o p c n -> (o p) c n")
                                             ).then_inc(wg_in, 16)
                        load(0, True)
                        with sp.Fori(1, LB) as b:
                            load(b, False)

                    @block.scalar
                    def _(a):
                        for s in (tr_ok, ti_ok, y2_ok):
                            a.sem_inc(s, 1)
                        a.wait_ge(e_in, 1)
                        a.activation(flat(z_[:, :, :]), flat(z_[:, :, :]), ACT.Exp, scale=-1.0).then_inc(e_ok, 1)
                        a.wait_ge(c_ok, 1)

                        def gates(b, o, d):
                            g = 4 * b + 2 * o + d
                            k = bass.ds(2 * b + o, 1)
                            a.wait_ge(r_ps, g + 1)
                            a.activation(tr[:, :], SA[:, 0:N], ACT.Tanh, bias=bg[:, 2 * d, k], scale=0.5).then_inc(tr_ok, 1)
                            a.wait_ge(i_ps, g + 2)
                            a.wait_ge(hd_ok, g + 1)
                            a.activation(ti[d][:, :], SB[:, 0:N], ACT.Tanh, bias=bg[:, 2 * d + 1, k], scale=0.5).then_inc(ti_ok, 1)
                            a.wait_ge(tr_ok, g + 2)
                            a.activation(aa[d][:, :], tr[:, :], ACT.Exp, bias=nc1[:, d, k], scale=nc1[:, d, k]).then_inc(a_ok, 1)
                            a.activation(qq[d][:, :], tr[:, :], ACT.Tanh, bias=c1[:, d, k], scale=c1[:, d, k]).then_inc(t2_ok, 1)
                            a.wait_ge(a_ok, g + 1)
                            a.wait_ge(t2_ok, g + 1)

                        def roots(b, o):
                            for d in range(2):
                                g = 4 * b + 2 * o + d
                                a.wait_ge(q_ok, g + 1)
                                a.activation(qq[d][:, :], qq[d][:, :], ACT.Sqrt).then_inc(sq_ok, 1)

                        def gelu_in(b, o):
                            n = 2 * b + o
                            k = bass.ds(n, 1)
                            a.wait_ge(y_ps, n + 1)
                            a.wait_ge(z_ok, n + 1)
                            a.activation(yb[:, :], banks(6, 2), ACT.Identity, bias=bin_[:, 0, k]).then_inc(y_ok, 1)
                            a.activation(y2[:, :], banks(6, 2), ACT.Square, bias=bin_[:, 0, k]).then_inc(y2_ok, 1)
                            a.wait_ge(gi_ok, n + 1)
                            a.activation(y2[:, :], y2[:, :], ACT.Tanh, scale=(2.0 / np.pi) ** 0.5).then_inc(gt_ok, 1)

                        with a.Fori(0, LB) as b:
                            for o, src in enumerate((SA, SB)):
                                n = 2 * b + o
                                a.wait_ge(u_ps, n + 1)
                                a.wait_ge(pad_ok, n + 1)
                                bias = bin_[:, 1, bass.ds(n, 1)]
                                a.activation(UP[o][:, LAT0:LAT0 + L], src[:, 0:L], ACT.Identity, bias=bias).then_inc(up_ok, 1)
                                a.activation(UP[o][:, CTX0:CTX0 + C], src[:, L:N], ACT.Identity, bias=bias).then_inc(up_ok, 1)
                            gelu_in(b, 0)
                            gates(b, 0, 0)
                            gates(b, 0, 1)
                            roots(b, 0)
                            gelu_in(b, 1)
                            gates(b, 1, 0)
                            gates(b, 1, 1)
                            roots(b, 1)

                    @block.vector
                    def _(v):
                        n_ = [0]

                        def once(ins):
                            n_[0] += 1
                            ins.then_inc(c_once, 1)
                            v.wait_ge(c_once, n_[0])

                        v.wait_ge(p_in, 80)
                        L2 = lambda x: flat(x[:, :, :])
                        once(v.tensor_scalar(L2(s_), L2(lam), -1.0, 0.0, ALU.mult, ALU.max))
                        once(v.tensor_scalar(L2(s2), L2(lam), 0.0, None, ALU.max))
                        v.tensor_tensor(L2(z_), L2(s_), L2(s2), ALU.add).then_inc(e_in, 1)
                        v.wait_ge(e_ok, 1)
                        once(v.tensor_scalar(L2(s2), L2(z_), 2.0, None, ALU.add))
                        once(v.reciprocal(L2(s2), L2(s2)))
                        once(v.tensor_tensor(L2(z_), L2(z_), L2(s2), ALU.mult))
                        once(v.tensor_tensor(L2(s2), L2(z_), L2(z_), ALU.mult))
                        once(v.memset(L2(acc), 1.0 / 17))
                        for m in range(15, 0, -2):
                            once(v.tensor_tensor(L2(acc), L2(acc), L2(s2), ALU.mult))
                            once(v.tensor_scalar(L2(acc), L2(acc), 1.0 / m, None, ALU.add))
                        once(v.tensor_tensor(L2(acc), L2(acc), L2(z_), ALU.mult))
                        once(v.scalar_tensor_tensor(out=L2(acc), in0=L2(acc), scalar=2.0, in1=L2(s_), op0=ALU.mult, op1=ALU.add))
                        once(v.tensor_scalar(L2(c1), L2(acc), 4.0, None, ALU.mult))
                        once(v.tensor_scalar(L2(nc1), L2(acc), -4.0, None, ALU.mult))
                        once(v.tensor_scalar(flat(bg[:, :, :]), flat(bg[:, :, :]), 0.5, None, ALU.mult))
                        for o in range(2):
                            once(v.memset(UP[o][:, :], 0.0))
                            v.sem_inc(pad_ok, 1)
                        v.sem_inc(c_ok, 1)
                        v.sem_inc(z_ok, 1)
                        v.sem_inc(hd_ok, 1)
                        v.sem_inc(hd_ok, 1)

                        def conv(b, o, link):
                            n = 2 * b + o
                            k = bass.ds(n, 1)
                            v.wait_ge(up_ok, 2 * n + 2)
                            link(v.tensor_scalar(cv[:, :], UP[o][:, 0:CVW], cw[:, 0, k], cb[:, k], ALU.mult, ALU.add))
                            for w in range(1, CW - 1):
                                link(v.scalar_tensor_tensor(out=cv[:, :], in0=UP[o][:, w:w + CVW], scalar=cw[:, w, k],
                                                            in1=cv[:, :], op0=ALU.mult, op1=ALU.add))
                            w = CW - 1
                            v.wait_ge(i_ps, 4 * b + 1)
                            link(v.scalar_tensor_tensor(out=uT[o][:, 0:L], in0=UP[o][:, w:w + L], scalar=cw[:, w, k],
                                                        in1=cv[:, 0:L], op0=ALU.mult, op1=ALU.add))
                            c0 = L + CW - 1
                            link(v.scalar_tensor_tensor(out=uT[o][:, L:N], in0=UP[o][:, w + c0:w + c0 + C], scalar=cw[:, w, k],
                                                        in1=cv[:, c0:c0 + C], op0=ALU.mult, op1=ALU.add))
                            v.sem_inc(pad_ok, 1)
                            v.sem_inc(u_ok, 1)

                        def gelu_mid(b, o, link):
                            n = 2 * b + o
                            v.wait_ge(y2_ok, n + 2)
                            link(v.tensor_scalar(y2[:, :], y2[:, :], 0.044715, 1.0, ALU.mult, ALU.add))
                            v.wait_ge(y_ok, n + 1)
                            v.tensor_tensor(y2[:, :], y2[:, :], yb[:, :], ALU.mult).then_inc(gi_ok, 1)

                        def decay(b, o, d, link):
                            g = 4 * b + 2 * o + d
                            v.wait_ge(a_ok, g + 1)
                            link(v.tensor_tensor(hh[d][:, :], aa[d][:, :], aa[d][:, :], ALU.mult))
                            v.wait_ge(t2_ok, g + 1)
                            v.scalar_tensor_tensor(out=qq[d][:, :], in0=hh[d][:, :], scalar=1.0, in1=qq[d][:, :],
                                                   op0=ALU.add, op1=ALU.mult).then_inc(q_ok, 1)
                            v.wait_ge(ti_ok, g + 2)
                            link(v.scalar_tensor_tensor(out=ti[d][:, :], in0=ti[d][:, :], scalar=1.0, in1=uT[o][:, :],
                                                        op0=ALU.add, op1=ALU.mult))

                        def scan(b, o, d, link):
                            g = 4 * b + 2 * o + d
                            v.wait_ge(sq_ok, g + 1)
                            v.wait_ge(a_ok, g + 1)
                            link(v.scalar_tensor_tensor(out=qq[d][:, :], in0=ti[d][:, :], scalar=0.5, in1=qq[d][:, :],
                                                        op0=ALU.mult, op1=ALU.mult))
                            turn = back if d else (lambda ap: ap)
                            link(v.tensor_tensor_scan(turn(hh[d][:, L:N]), turn(aa[d][:, L:N]), turn(qq[d][:, L:N]), 0.0,
                                                      ALU.mult, ALU.add))
                            end = L if d else N - 1
                            link(v.tensor_tensor_scan(turn(hh[d][:, 0:L]), turn(aa[d][:, 0:L]), turn(qq[d][:, 0:L]),
                                                      hh[d][:, end:end + 1], ALU.mult, ALU.add))
                            v.sem_inc(hd_ok, 1)

                        def close(b, o, link):
                            n = 2 * b + o
                            link(v.tensor_tensor(hh[0][:, 0:L], hh[0][:, 0:L], hh[1][:, 0:L], ALU.add))
                            v.wait_ge(gt_ok, n + 1)
                            link(v.scalar_tensor_tensor(out=y2[:, :], in0=y2[:, :], scalar=1.0, in1=yb[:, :],
                                                        op0=ALU.add, op1=ALU.mult))
                            v.scalar_tensor_tensor(out=zT[:, bass.ds(n, 1), :].rearrange("p o n -> p (o n)"), in0=y2[:, :],
                                                   scalar=0.5, in1=hh[0][:, 0:L], op0=ALU.mult, op1=ALU.mult).then_inc(z_ok, 1)

                        with v.Fori(0, LB) as b:
                            link = Chain(v, dv, 2 * (5 + 1 + 2 * 2 + 2 * 3 + 2), b)
                            conv(b, 0, link)
                            conv(b, 1, link)
                            for o in range(2):
                                gelu_mid(b, o, link)
                                decay(b, o, 0, link)
                                decay(b, o, 1, link)
                                scan(b, o, 0, link)
                                scan(b, o, 1, link)
                                close(b, o, link)
                            link.end()

                    @block.tensor
                    def _(t):
                        def product(n, w, o, dst, cols, s):
                            for c in range(0, cols, 512):
                                wd = min(512, cols - c)
                                for k in range(KD):
                                    mm = t.matmul(dst[:, c:c + wd], w[:, k, o * P:(o + 1) * P], hT[:, k, c:c + wd],
                                                  start=(k == 0), stop=(k == KD - 1))
                            mm.then_inc(s, 1)

                        def gates(b, o, d):
                            g = 4 * b + 2 * o + d
                            for q, dst, free, s in ((2 * d, SA, tr_ok, r_ps), (2 * d + 1, SB, ti_ok, i_ps)):
                                t.wait_ge(free, g + 1)
                                for c in range(0, N, 512):
                                    wd = min(512, N - c)
                                    for k in range(2):
                                        mm = t.matmul(dst[:, c:c + wd], wg[:, q, k, o * P:(o + 1) * P], uT[k][:, c:c + wd],
                                                      start=(k == 0), stop=(k == 1))
                                mm.then_inc(s, 1)

                        t.sem_inc(i_ps, 1)
                        with t.Fori(0, LB) as b:
                            t.wait_ge(wu_in, 16 * b + 16)
                            t.wait_ge(tr_ok, 4 * b + 1)
                            product(2 * b, wu, 0, SA, N, u_ps)
                            t.wait_ge(ti_ok, 4 * b + 1)
                            product(2 * b + 1, wu, 1, SB, N, u_ps)
                            t.wait_ge(wy_in, 16 * b + 16)
                            t.wait_ge(y2_ok, 2 * b + 1)
                            product(2 * b, wy, 0, banks(6, 2), L, y_ps)
                            t.wait_ge(wg_in, 64 * b + 64)
                            t.wait_ge(u_ok, 2 * b + 2)
                            t.wait_ge(up_ok, 4 * b + 4)
                            gates(b, 0, 0)
                            gates(b, 0, 1)
                            t.wait_ge(y2_ok, 2 * b + 2)
                            product(2 * b + 1, wy, 1, banks(6, 2), L, y_ps)
                            gates(b, 1, 0)
                            gates(b, 1, 1)

        def routing_tables(stack, l, nt):
            return (sbuf(stack, f"dst{l}", [P, 2, nt], I32), sbuf(stack, f"w01_{l}", [P, 2, nt]),
                    sbuf(stack, f"item{l}", [P, ITEMS], I32), sbuf(stack, f"item_slots{l}", [P, ITEMS], I32),
                    sbuf(stack, f"n_pairs{l}", [P, 1], I32))

        with ExitStack() as layer:
            RL = sbuf(layer, "RL0", [P, NT, NR])
            tabs = routing_tables(layer, 0, NT)
            with ExitStack() as att:
                OT = sbuf(att, "OT", [P, KD, N])
                with ExitStack() as sth:
                    hT = sbuf(sth, "hT", [P, KD, N])
                    first_norm(hT)
                    if stop == 1:
                        return
                    attention(hT, OT)
                    if stop == 2:
                        return
                projection(0, NT, OT, A["na_w_o"][0], A["na_b_o"][0], RL)
                if stop == 3:
                    return
            ng = sbuf(layer, "ng", [P, D])
            routing(0, NT, RL, tabs, ng)
            if stop == 4:
                return
            experts(0, tabs)
            if stop == 5:
                return
            RL1 = sbuf(layer, "RL1", [P, NTL, NR])
            tabs1 = routing_tables(layer, 1, NTL)
            with ExitStack() as lru:
                zT = sbuf(lru, "zT", [P, KD, L])
                with ExitStack() as sth:
                    hT = sbuf(sth, "hT1", [P, KD, N])
                    combine(0, NT, tabs, ng, hT)
                    semaphores_anew()
                    if stop == 6:
                        return
                    recurrent(hT, zT, ng)
                    if stop == 7:
                        return
                projection(1, NTL, zT, A["lru_w_o"][0], A["lru_b_o"][0], RL1)
                if stop == 8:
                    return
            routing(1, NTL, RL1, tabs1, ng)
            experts(1, tabs1)
            combine(1, NTL, tabs1, ng, None)


_INS = ["x", "c", "ctx", "c_ctx", "ada_w", "ada_b", "norm_g", "na_w_qkv", "na_b_qkv", "na_rpb", "na_w_o", "na_b_o",
        "lru_w_in", "lru_b_in", "lru_conv_w", "lru_conv_b", "lru_w_gate", "lru_b_gate", "lru_lambda", "lru_w_o",
        "lru_b_o", "moe_w_group", "moe_b_group", "moe_w_expert", "moe_b_expert", "moe_w1", "moe_w3", "moe_w2", "final_g"]


def kernel(**inputs):
    import concourse.bacc as bacc
    from concourse.bass_utils import run_bass_kernel_spmd

    nc = bacc.Bacc("TRN2", target_bir_lowering=False, num_devices=1)
    arrays, aps = {}, {}
    for name in _INS:
        a = np.ascontiguousarray(inputs[name])
        if name == "na_rpb":
            side = (RPB_W - a.shape[-1]) // 2
            a = np.pad(a, ((0, 0), (0, 0), (0, 0), (side, side)))
        arrays[f"in_{name}"] = a
        aps[name] = nc.dram_tensor(f"in_{name}", a.shape, F32, kind="ExternalInput").ap()
    out = nc.dram_tensor("out", (1, L, D), F32, kind="ExternalOutput").ap()
    program(nc, aps, out)
    r = run_bass_kernel_spmd(nc, [arrays], core_ids=[0])
    return r.results[0]["out"]
```
